# Optimizing a Trainium2 kernel written in Bass

```python
import math
import jax
import jax.numpy as jnp
from jax import lax
import numpy as np

D_MODEL = 1024
BATCH = 1
SEQ = 512
DEPTH = 1

CHUNK = 64
N_BACK = 8
BAND = (N_BACK + 1) * CHUNK
N_HEADS = 8
HEAD_DIM = 64
ATTN_WIDTH = N_HEADS * HEAD_DIM
REL_CLIP = 256
SG_BLOCK = 128
SG_GROUPS = 4
SG_WIDTH = 512
SG_GROUP_DIM = SG_WIDTH // SG_GROUPS
IN_WIDTH = 3 * ATTN_WIDTH + 2 * SG_WIDTH + 2 * D_MODEL
N_EXPERTS = 32
TOP_K = 4
D_FF = D_MODEL
SWIGLU_LIMIT = 7.0
SWIGLU_ALPHA = 1.702
MOE_BLOCK = 128
EPS = 1e-6

kernel_name = "chunked_attn_gmlp_gated_moe_block"

def rms_norm(x, g):
    xf = x.astype(jnp.float32)
    y = xf * lax.rsqrt(jnp.mean(xf * xf, axis=-1, keepdims=True) + EPS)
    return (y * g.astype(jnp.float32)).astype(x.dtype)

def layer_norm(x, g, b):
    xf = x.astype(jnp.float32)
    mu = jnp.mean(xf, axis=-1, keepdims=True)
    xc = xf - mu
    y = xc * lax.rsqrt(jnp.mean(xc * xc, axis=-1, keepdims=True) + EPS)
    return (y * g.astype(jnp.float32) + b.astype(jnp.float32)).astype(x.dtype)

def rel_index():
    qi = np.arange(CHUNK)[:, None] + N_BACK * CHUNK
    kk = np.arange(BAND)[None, :]
    return np.clip(qi - kk, -REL_CLIP, REL_CLIP) + REL_CLIP

def chunked_attention(q, k, v, rel_bias):
    B, S, H, Dh = q.shape
    n_chunks = S // CHUNK
    pad = N_BACK * CHUNK
    kp = jnp.pad(k, ((0, 0), (pad, 0), (0, 0), (0, 0)))
    vp = jnp.pad(v, ((0, 0), (pad, 0), (0, 0), (0, 0)))
    bias = rel_bias.astype(jnp.float32)[:, rel_index()]
    kk = jnp.arange(BAND)
    scale = 1.0 / math.sqrt(Dh)

    def one_chunk(n):
        qs = lax.dynamic_slice_in_dim(q, n * CHUNK, CHUNK, axis=1)
        ks = lax.dynamic_slice_in_dim(kp, n * CHUNK, BAND, axis=1)
        vs = lax.dynamic_slice_in_dim(vp, n * CHUNK, BAND, axis=1)
        s = jnp.einsum('bqhd,bkhd->bhqk', qs, ks).astype(jnp.float32) * scale + bias
        valid = kk >= (N_BACK - n) * CHUNK
        s = jnp.where(valid, s, -1e30)
        p = jax.nn.softmax(s, axis=-1).astype(v.dtype)
        return jnp.einsum('bhqk,bkhd->bqhd', p, vs)

    out = lax.map(one_chunk, jnp.arange(n_chunks))
    return out.transpose(1, 0, 2, 3, 4).reshape(B, S, H * Dh)

def spatial_gating(u, v, ln_g, ln_b, w_s, b_s):
    B, S, _ = u.shape
    vg = v.reshape(B, S // SG_BLOCK, SG_BLOCK, SG_GROUPS, SG_GROUP_DIM)
    vn = layer_norm(vg, ln_g.reshape(SG_GROUPS, SG_GROUP_DIM), ln_b.reshape(SG_GROUPS, SG_GROUP_DIM))
    mask = jnp.tril(jnp.ones((SG_BLOCK, SG_BLOCK), w_s.dtype))
    mixed = jnp.einsum('gts,bnsgc->bntgc', w_s * mask, vn) + b_s.T[:, :, None]
    return u * mixed.reshape(B, S, SG_WIDTH)

def clamped_swiglu(gu):
    gate, up = jnp.split(gu, 2, axis=-1)
    gate = jnp.minimum(gate, SWIGLU_LIMIT)
    up = jnp.clip(up, -SWIGLU_LIMIT, SWIGLU_LIMIT)
    return (up + 1.0) * (gate * jax.nn.sigmoid(gate * SWIGLU_ALPHA))

def moe(h, router_w, router_b, w_gate_up, b_gate_up, w_down, b_down):
    T, D = h.shape
    logits = (h @ router_w + router_b).astype(jnp.float32)
    top_v, top_i = lax.top_k(logits, TOP_K)
    probs = jax.nn.softmax(top_v, axis=-1)
    n_assign = T * TOP_K
    e_flat = top_i.reshape(n_assign)
    tok_flat = jnp.arange(n_assign, dtype=jnp.int32) // TOP_K
    order = jnp.argsort(e_flat)
    e_sorted = e_flat[order]
    tok_sorted = tok_flat[order]
    w_sorted = probs.reshape(n_assign)[order]
    counts = jnp.zeros((N_EXPERTS,), jnp.int32).at[e_flat].add(1)
    starts = jnp.cumsum(counts) - counts
    padded = (counts + MOE_BLOCK - 1) // MOE_BLOCK * MOE_BLOCK
    pends = jnp.cumsum(padded)
    pstarts = pends - padded
    rank = jnp.arange(n_assign, dtype=jnp.int32) - starts[e_sorted]
    dest = pstarts[e_sorted] + rank
    n_slots = n_assign + N_EXPERTS * MOE_BLOCK
    n_blocks = n_slots // MOE_BLOCK
    slot_tok = jnp.full((n_slots,), T, jnp.int32).at[dest].set(tok_sorted)
    h_pad = jnp.concatenate([h, jnp.zeros((1, D), h.dtype)], axis=0)
    x_slots = h_pad[slot_tok].reshape(n_blocks, MOE_BLOCK, D)
    blk_start = jnp.arange(n_blocks, dtype=jnp.int32) * MOE_BLOCK
    blk_expert = jnp.minimum(jnp.searchsorted(pends, blk_start, side='right'), N_EXPERTS - 1)

    def expert_block(args):
        xb, e = args
        gu = xb @ w_gate_up[e] + b_gate_up[e]
        return clamped_swiglu(gu) @ w_down[e] + b_down[e]

    y_slots = lax.map(expert_block, (x_slots, blk_expert)).reshape(n_slots, D)
    y_assign = y_slots[dest] * w_sorted[:, None].astype(h.dtype)
    return jnp.zeros((T, D), h.dtype).at[tok_sorted].add(y_assign)

def setup_inputs(seed: int = 0) -> dict:
    key = jax.random.key(seed)
    ks = jax.random.split(key, 24)
    f32 = jnp.float32

    def nrm(k, shape, scale):
        return jax.random.normal(k, shape, f32) * scale

    return {
        "x": nrm(ks[0], (BATCH, SEQ, D_MODEL), 1.0),
        "norm1_g": 1.0 + nrm(ks[1], (DEPTH, D_MODEL), 0.02),
        "w_in": nrm(ks[2], (DEPTH, D_MODEL, IN_WIDTH), D_MODEL ** -0.5),
        "q_norm_g": 1.0 + nrm(ks[3], (DEPTH, HEAD_DIM), 0.02),
        "k_norm_g": 1.0 + nrm(ks[4], (DEPTH, HEAD_DIM), 0.02),
        "rel_bias": nrm(ks[5], (DEPTH, N_HEADS, 2 * REL_CLIP + 1), 0.5),
        "sg_ln_g": 1.0 + nrm(ks[6], (DEPTH, SG_WIDTH), 0.02),
        "sg_ln_b": nrm(ks[7], (DEPTH, SG_WIDTH), 0.02),
        "sg_w": nrm(ks[8], (DEPTH, SG_GROUPS, SG_BLOCK, SG_BLOCK), SG_BLOCK ** -0.5),
        "sg_b": 1.0 + nrm(ks[9], (DEPTH, SG_GROUPS, SG_BLOCK), 0.02),
        "w_branch_a": nrm(ks[10], (DEPTH, ATTN_WIDTH, D_MODEL), ATTN_WIDTH ** -0.5),
        "w_branch_b": nrm(ks[11], (DEPTH, SG_WIDTH, D_MODEL), SG_WIDTH ** -0.5),
        "w_out": nrm(ks[12], (DEPTH, D_MODEL, D_MODEL), D_MODEL ** -0.5),
        "norm2_g": 1.0 + nrm(ks[13], (DEPTH, D_MODEL), 0.02),
        "router_w": nrm(ks[14], (DEPTH, D_MODEL, N_EXPERTS), D_MODEL ** -0.5),
        "router_b": nrm(ks[15], (DEPTH, N_EXPERTS), 0.01),
        "w_gate_up": nrm(ks[16], (DEPTH, N_EXPERTS, D_MODEL, 2 * D_FF), D_MODEL ** -0.5),
        "b_gate_up": nrm(ks[17], (DEPTH, N_EXPERTS, 2 * D_FF), 0.01),
        "w_down": nrm(ks[18], (DEPTH, N_EXPERTS, D_FF, D_MODEL), D_FF ** -0.5),
        "b_down": nrm(ks[19], (DEPTH, N_EXPERTS, D_MODEL), 0.01),
    }

def reference(x, norm1_g, w_in, q_norm_g, k_norm_g, rel_bias, sg_ln_g, sg_ln_b, sg_w, sg_b,
              w_branch_a, w_branch_b, w_out, norm2_g, router_w, router_b,
              w_gate_up, b_gate_up, w_down, b_down):
    B, S, D = x.shape
    cuts = np.cumsum([ATTN_WIDTH, ATTN_WIDTH, ATTN_WIDTH, SG_WIDTH, SG_WIDTH, D_MODEL]).tolist()
    for l in range(DEPTH):
        h = rms_norm(x, norm1_g[l])
        proj = jnp.einsum('bsd,de->bse', h, w_in[l])
        q, k, v, u_sg, v_sg, g_a, g_b = jnp.split(proj, cuts, axis=-1)
        q = rms_norm(q.reshape(B, S, N_HEADS, HEAD_DIM), q_norm_g[l])
        k = rms_norm(k.reshape(B, S, N_HEADS, HEAD_DIM), k_norm_g[l])
        v = v.reshape(B, S, N_HEADS, HEAD_DIM)
        y_attn = chunked_attention(q, k, v, rel_bias[l])
        y_sg = spatial_gating(jax.nn.gelu(u_sg), jax.nn.gelu(v_sg),
                              sg_ln_g[l], sg_ln_b[l], sg_w[l], sg_b[l])
        merged = (jax.nn.sigmoid(g_a) * (y_attn @ w_branch_a[l])
                  + jax.nn.sigmoid(g_b) * (y_sg @ w_branch_b[l]))
        x = x + merged @ w_out[l]
        h2 = rms_norm(x, norm2_g[l]).reshape(B * S, D)
        x = x + moe(h2, router_w[l], router_b[l], w_gate_up[l], b_gate_up[l],
                    w_down[l], b_down[l]).reshape(B, S, D)
    return x


_drawn_inputs = setup_inputs


def setup_inputs(seed=0):
    import zlib

    import numpy as np

    out = dict(_drawn_inputs(seed))
    spreads = {}
    factors = {'q_norm_g': 3.838,
     'k_norm_g': 4.602,
     'sg_ln_g': 2.678,
     'sg_ln_b': 8.988,
     'sg_b': 2.817,
     'b_gate_up': 8.0,
     'b_down': 8.0,
     'router_b': 3.766}
    for name, (base, spread) in spreads.items():
        noise = np.random.default_rng([zlib.crc32(name.encode()), seed]).standard_normal(out[name].shape)
        drawn = base * np.exp(spread * noise) if base else spread * noise
        out[name] = jnp.asarray(drawn.astype(out[name].dtype))
    for name, factor in factors.items():
        out[name] = (out[name] * factor).astype(out[name].dtype)
    return out
```

```python
from contextlib import ExitStack

import concourse.bass as bass
from concourse import mybir

ALU = mybir.AluOpType
ACT = mybir.ActivationFunctionType
AX_X = mybir.AxisListType.X
F32 = mybir.dt.float32
I32 = mybir.dt.int32
U32 = mybir.dt.uint32

P = 128
SLOTS = 12
CHUNK = 2048
REG = 2048
NEG = -1e30


def block_kernel(nc, x, norm1_g, w_in, q_norm_g, k_norm_g, rel_bias, sg_ln_g, sg_ln_b, sg_w, sg_b,
                 w_branch_a, w_branch_b, w_out, norm2_g, router_w, router_b,
                 w_gate_up, b_gate_up, w_down, b_down, out):
    _, S, D = x.shape
    H, REL = rel_bias.shape[1:]
    DH = q_norm_g.shape[1]
    G = sg_w.shape[1]
    SGW = sg_ln_g.shape[1]
    AW = H * DH
    E = router_w.shape[2]
    FF = w_down.shape[2]
    TOPK = 4
    CLIP = (REL - 1) // 2
    LIMIT, ALPHA, EPS = 7.0, 1.702, 1e-6
    T = S // P
    KD = D // P
    FT = FF // P
    HP = H // 2
    SIZES = (64, 96, 128)
    EXTRA = S * TOPK // P - 1
    PAIRC = 256
    assert T == 4 and KD == 8 and FT == 8 and AW == 512 and SGW == 512 and DH == 64 and G == 4

    UNITS = 8 + 4 + 8 + 8 + 4
    U_BASE, B_BASE, A_BASE, O_BASE = 8, 12, 20, 28
    q0, u0 = 0, 3 * AW
    v0 = u0 + SGW
    ga0, gb0 = u0 + 2 * SGW, u0 + 2 * SGW + D
    chunks = []
    for c in range(6):
        chunks.append(("in", q0 + c * PAIRC, c + 1))
    for c in range(2):
        chunks.append(("in", v0 + c * PAIRC, 7 + c))
    for c in range(2):
        chunks.append(("in", u0 + c * PAIRC, U_BASE + 2 * c + 2))
    for kind, base, col in (("b", B_BASE, gb0), ("a", A_BASE, ga0)):
        for half in range(2):
            chunks.append((kind, half * 512, base + 4 * half + 4))
            for c in range(2):
                chunks.append(("in", col + (2 * half + c) * PAIRC, base + 4 * half + 2 * c + 2))
    for c in range(4):
        chunks.append(("o", c * PAIRC, O_BASE + c + 1))
    DENSE = len(chunks)
    SHIFT = SLOTS - DENSE % SLOTS

    def slot(c):
        return (c + SHIFT) % SLOTS

    def uses(c):
        return sum(slot(b) == slot(c) for b in range(c + 1))

    SLOT_USES = [sum(slot(b) == j for b in range(DENSE)) for j in range(SLOTS)]

    def in_chunk(n):
        return [c for c, (kind, _, _) in enumerate(chunks) if kind == "in"][n]

    UNIT_CHUNK = {}
    for u in range(8):
        UNIT_CHUNK[u] = in_chunk(u)
    for u in range(U_BASE, O_BASE):
        UNIT_CHUNK[u] = in_chunk(8 + (u - U_BASE) // 2)
    for u in range(O_BASE, UNITS):
        UNIT_CHUNK[u] = DENSE - 4 + u - O_BASE
    BRANCH_CHUNK = {(kind, half): [c for c, (k, _, _) in enumerate(chunks) if k == kind][half]
                    for kind in "ab" for half in range(2)}

    h2_rows = nc.dram_tensor("h2_rows", (S, D), F32, kind="Internal").ap()
    rel_rows = nc.dram_tensor("rel_rows", (H, 5 * P), F32, kind="Internal").ap()

    gu_rows = w_gate_up.rearrange("l e k n -> (l e k) n")
    down_rows = w_down.rearrange("l e k n -> (l e k) n")
    out_rows = out.rearrange("b s d -> (b s) d")
    x_rows = x.rearrange("b s d -> (b s) d")

    with ExitStack() as ctx:
        def sb(name, shape, dt=F32):
            return ctx.enter_context(nc.sbuf_tensor(name, shape, dt))

        def sem(name):
            return ctx.enter_context(nc.semaphore(name))

        ring = sb("ring", [P, SLOTS, CHUNK])
        work = sb("work", [P, 13 * REG])

        def region(r, off, n):
            return work[:, r * REG + off:r * REG + off + n]

        xin = region(0, 0, 2 * REG).rearrange("p (t d) -> p t d", t=T)
        qk_rows = [region(r, 0, REG).rearrange("p (t n) -> p t n", t=T) for r in (0, 1)]
        merged = region(0, 0, 2 * REG).rearrange("p (m s) -> p m s", m=KD)
        hT = region(2, 0, 2 * REG).rearrange("p (k s) -> p k s", k=KD)
        x2 = region(2, 0, 2 * REG).rearrange("p (t d) -> p t d", t=T)
        qT = region(4, 0, REG).rearrange("p (h s) -> p h s", h=HP)
        kT = region(5, 0, REG).rearrange("p (h s) -> p h s", h=HP)
        vv = region(6, 0, REG).rearrange("p (t n) -> p t n", t=T)
        vn = region(7, 0, REG).rearrange("p (t n) -> p t n", t=T)
        uT = region(8, 0, REG).rearrange("p (g s) -> p g s", g=G)
        relM = region(9, 0, 1024).rearrange("p (b n) -> p b n", b=2)
        srow = region(9, 1024, 1024).rearrange("p (b n) -> p b n", b=2)
        prow = region(10, 0, 1024).rearrange("p (b n) -> p b n", b=2)
        pcol = region(10, 1024, 1024).rearrange("p (b n) -> p b n", b=2)
        scratch = region(11, 0, 1024)
        bias_rows = region(11, 1024, 768).rearrange("p (c n) -> p c n", c=6)
        gate = region(11, 0, 1024).rearrange("p (b n) -> p b n", b=2)
        gated = region(11, 1024, 512)
        ln_g = region(12, 0, 512)
        ln_b = region(12, 512, 512)
        sgb = region(12, 1024, 512).rearrange("p (g n) -> p g n", g=G)
        wT = region(12, 1536, 512).rearrange("p (g n) -> p g n", g=G)
        sgw_rows = region(10, 0, 512).rearrange("p (g n) -> p g n", g=G)
        rel_in = region(9, 1024, REL)
        rel_out = region(10, 1024, 5 * P)
        g2 = region(12, 0, 1024)
        rw = region(12, 1024, KD * E).rearrange("p (k e) -> p k e", k=KD)
        h2 = region(4, 0, 2 * REG).rearrange("p (t d) -> p t d", t=T)
        h2T = region(6, 0, 2 * REG).rearrange("p (k s) -> p k s", k=KD)
        rt = region(0, 0, 2 * REG)
        TE = T * E
        logits, chosen, weight, hit, before, place_a = (
            rt[:, n * TE:(n + 1) * TE].rearrange("p (t e) -> p t e", t=T) for n in range(6))
        rb_all = rt[:, 6 * TE:6 * TE + E]
        iota_e = rt[:, 6 * TE + E:6 * TE + 2 * E]
        top = rt[:, 1024:1024 + 8 * T].rearrange("p (t k) -> p t k", t=T)
        top_i = rt[:, 1056:1056 + 8 * T].rearrange("p (t k) -> p t k", t=T).bitcast(U32)
        top_f = rt[:, 1088:1088 + 8 * T].rearrange("p (t k) -> p t k", t=T)
        prob = rt[:, 1120:1120 + TOPK * T].rearrange("p (t k) -> p t k", t=T)
        psum_t = rt[:, 1140:1140 + T]
        neg_t = rt[:, 1144:1144 + T]
        col_cnt = rt[0:E, 1150:1151]
        col_fl = rt[0:E, 1152:1155]
        col_nb = rt[0:E, 1156:1157]
        col_base = rt[0:E, 1158:1159]
        col_eb = rt[0:E, 1160:1162]
        col_code = rt[0:E, 1164:1165]
        oh_x = rt[0:E, 1170:1170 + 3 * (EXTRA + 1)].rearrange("p (b j) -> p b j", b=3)
        xg = region(9, 0, 1024)
        yrow = region(9, 1024, 1024)
        xT = region(10, 0, 1024).rearrange("p (k n) -> p k n", k=KD)
        hh = region(10, 1024, 1024).rearrange("p (m n) -> p m n", m=FT)
        eg = region(11, 0, 1024).rearrange("p (m n) -> p m n", m=FT)
        eu = region(11, 1024, 1024).rearrange("p (m n) -> p m n", m=FT)
        es = region(7, 0, 1024).rearrange("p (m n) -> p m n", m=FT)
        iota_s = region(8, 0, 512)
        onehot = region(8, 512, 512).rearrange("p (t n) -> p t n", t=T)
        yT = region(8, 1024, 1024).rearrange("p (m n) -> p m n", m=KD)

        ident = sb("ident", [P, P])
        ones = sb("ones", [P, P])
        before_m = sb("before_m", [P, P])
        rows = sb("rows", [P, P])
        colT = sb("colT", [P, 10])
        biasT = sb("biasT", [P, E * 2 * FT + E * KD])
        bguT, bdT = biasT[:, 0:E * 2 * FT], biasT[:, E * 2 * FT:]
        eps = sb("eps", [P, 1])
        stat = sb("stat", [P, 16])
        rstd = sb("rstd", [P, 16])
        mean = sb("mean", [P, 8])
        smax = sb("smax", [P, 2])
        nmax = sb("nmax", [P, 2])
        ssum = sb("ssum", [P, 2])
        rsum = sb("rsum", [P, 2])
        pos = sb("pos", [P, T, E + 1])
        vals = sb("vals", [P, T, E + 1, 2])
        val_e = sb("val_e", [P, T, 2])
        plan_i = sb("plan_i", [P, 2], I32)
        plan_w = sb("plan_w", [P, 2])
        tokn = sb("tokn", [P, T])
        table = sb("table", [1, 80], I32)
        N_AT, XE_AT, XB_AT, NX_AT = 0, E + 1, E + 1 + EXTRA + 1, E + 1 + 2 * (EXTRA + 1)

        PJ = ctx.enter_context(nc.psum_tensor("PJ", [P, 2, 1024], F32))
        SBK = ctx.enter_context(nc.psum_tensor("SBK", [P, 2, 512], F32))
        TT = ctx.enter_context(nc.psum_tensor("TT", [P, 1024], F32))
        PT, PV = TT[:, 0:512], TT[:, 512:1024]
        YD = SBK[:, :, :].rearrange("p b n -> p (b n)")

        arrived = [sem(f"arrived{j}") for j in range(SLOTS)]
        x_in = [sem(f"x_in{t}") for t in range(T)]
        rows_in, bias_in, sgw_in, rel_in_s, ln_in = (sem(n) for n in
            ("rows_in", "bias_in", "sgw_in", "rel_in_s", "ln_in"))
        rel_stored, relM_in, x_again, late_in = (sem(n) for n in ("rel_stored", "relM_in", "x_again", "late_in"))
        pool_made = sem("pool_made")
        sgw_masked = sem("sgw_masked")
        relM_ready = sem("relM_ready")
        cols_turned, cols_ready = sem("cols_turned"), sem("cols_ready")
        bias_turned, bias_ready = sem("bias_turned"), sem("bias_ready")
        sgw_turned, wT_ready = sem("sgw_turned"), sem("wT_ready")
        x_sq, xs_ready, x_turned, hT_ready = (sem(n) for n in ("x_sq", "xs_ready", "x_turned", "hT_ready"))
        rel_ready = sem("rel_ready")
        unit_ready = sem("unit_ready")
        unit_free = [sem(f"unit_free{b}") for b in range(2)]
        qk_sq, qk_var, qk_std = sem("qk_sq"), sem("qk_var"), sem("qk_std")
        qk_turned, qk_ready, v_ready = sem("qk_turned"), sem("qk_ready"), sem("v_ready")
        vg_ready, vc_ready, vc_sq, v_var, v_std, vn_ready = (sem(n) for n in
            ("vg_ready", "vc_ready", "vc_sq", "v_var", "v_std", "vn_ready"))
        u_ready, mixed, sgu_ready = sem("u_ready"), sem("mixed"), sem("sgu_ready")
        scores_ready, smax_ready, exp_ready, probs_ready = (sem(n) for n in
            ("scores_ready", "smax_ready", "exp_ready", "probs_ready"))
        probs_turned, pcol_ready, pv_done, attn_ready = (sem(n) for n in
            ("probs_turned", "pcol_ready", "pv_done", "attn_ready"))
        gate_ready, merged_ready = sem("gate_ready"), sem("merged_ready")
        x2_ready, x2_sq, x2_var, x2_std, h2_ready = (sem(n) for n in
            ("x2_ready", "x2_sq", "x2_var", "x2_std", "h2_ready"))
        h2_stored, out_stored = sem("h2_stored"), sem("out_stored")
        h2_turned, h2T_ready, logits_ready = sem("h2_turned"), sem("h2T_ready"), sem("logits_ready")
        top_ready, top_exp, chosen_ready, counted = (sem(n) for n in
            ("top_ready", "top_exp", "chosen_ready", "counted"))
        extra_cols, extra_base, extra_hot, extra_ready, routed = (sem(n) for n in
            ("extra_cols", "extra_base", "extra_hot", "extra_ready", "routed"))
        hot_ready, plan_there, plan_ready = sem("hot_ready"), sem("plan_there"), sem("plan_ready")
        gathered, xg_turned, xT_ready = sem("gathered"), sem("xg_turned"), sem("xT_ready")
        gu_ready, chunk_used, g_ready, s_ready, hh_ready = (sem(n) for n in
            ("gu_ready", "chunk_used", "g_ready", "s_ready", "hh_ready"))
        yd_ready, yT_ready, y_turned, y_ready, scattered = (sem(n) for n in
            ("yd_ready", "yT_ready", "y_turned", "y_ready", "scattered"))
        dve_chain, act_chain, waits_met = sem("dve_chain"), sem("act_chain"), sem("waits_met")

        def free_before(u):
            return u // 2

        def by_rows(eng, count, body):
            with eng.If(count < SIZES[0] + 1):
                body(SIZES[0])
            with eng.Else():
                with eng.If(count < SIZES[1] + 1):
                    body(SIZES[1])
                with eng.Else():
                    body(SIZES[2])
                eng.nop()

        def settle(eng):
            eng.sem_inc(waits_met, 1)

        def load(eng, at, most):
            return eng.value_load(table[0:1, bass.ds(at, 1)], min_val=0, max_val=most)

        block = ctx.enter_context(nc.Block())

        @block.sync
        def _(sp):
            for t in range(T):
                sp.dma_start(xin[:, t, :], x_rows[t * P:(t + 1) * P, :]).then_inc(x_in[t], 16)
            for c, (kind, col, _) in enumerate(chunks):
                if c >= SLOTS:
                    sp.wait_ge(unit_ready, chunks[c - SLOTS][2])
                if kind == "in":
                    src, n = w_in[0, :, col:col + PAIRC], PAIRC
                elif kind == "o":
                    src, n = w_out[0, :, col:col + PAIRC], PAIRC
                else:
                    src, n = (w_branch_a if kind == "a" else w_branch_b)[0, :, col:col + 512], 512
                sp.dma_start(ring[:, slot(c), :].rearrange("p (k n) -> p k n", n=n),
                             src.rearrange("(k p) n -> p k n", p=P)).then_inc(arrived[slot(c)], 16)

            def used(i, j):
                if j in (KD - 1, SLOTS - 1):
                    sp.wait_ge(gu_ready if j < KD else yd_ready, i * 2 + 2)
                else:
                    sp.wait_ge(chunk_used, i * (SLOTS - 2) + (j + 1 if j < KD else j))

            def expert_chunk(e, j):
                if j < KD:
                    sp.dma_start(ring[:, j, :], gu_rows[bass.ds(e * D + j * P, P), :]).then_inc(arrived[j], 16)
                else:
                    sp.dma_start(ring[:, j, :].rearrange("p (c n) -> p c n", c=2),
                                 down_rows[bass.ds(e * FF + (j - KD) * 2 * P, 2 * P), :]
                                 .rearrange("(c p) n -> p c n", p=P)).then_inc(arrived[j], 16)

            for j in range(SLOTS):
                sp.wait_ge(unit_ready, chunks[DENSE - SLOTS + j][2])
                expert_chunk(0, j)
            for t in range(T):
                sp.wait_ge(h2_ready, t + 1)
                sp.dma_start(h2_rows[t * P:(t + 1) * P, :], h2[:, t, :]).then_inc(h2_stored, 16)
                sp.dma_start(out_rows[t * P:(t + 1) * P, :], x2[:, t, :]).then_inc(out_stored, 16)
            with sp.Fori(1, E) as i:
                for j in range(SLOTS):
                    used(i - 1, j)
                    expert_chunk(i, j)
            sp.wait_ge(routed, 1)
            n_extra = load(sp, NX_AT, EXTRA)
            with sp.Fori(0, EXTRA) as b:
                with sp.If(b < n_extra):
                    e = load(sp, b + XE_AT, E - 1)
                    for j in range(SLOTS):
                        used(b + (E - 1), j)
                        expert_chunk(e, j)
                with sp.Else():
                    sp.nop()

        @block.gpsimd
        def _(pool):
            made = [0]

            def link(ins):
                made[0] += 1
                ins.then_inc(pool_made, 1)
                pool.wait_ge(pool_made, made[0])

            pool.dma_start(ln_g, sg_ln_g[0:1, :].to_broadcast([P, SGW])).then_inc(ln_in, 16)
            pool.dma_start(ln_b, sg_ln_b[0:1, :].to_broadcast([P, SGW])).then_inc(ln_in, 16)
            pool.dma_start(sgb.rearrange("p g n -> p (g n)"),
                           sg_b.rearrange("l g n -> l (g n)").to_broadcast([P, SGW])).then_inc(ln_in, 16)
            link(nc.gpsimd.memset(ident[:], 0.0))
            link(nc.gpsimd.memset(ones[:], 1.0))
            link(nc.gpsimd.affine_select(out=ident[:], in_=ident[:], compare_op=ALU.not_equal, fill=1.0,
                                         base=0, pattern=[[-1, P]], channel_multiplier=1))
            link(nc.gpsimd.affine_select(out=before_m[:], in_=ones[:], compare_op=ALU.is_gt, fill=0.0,
                                         base=0, pattern=[[1, P]], channel_multiplier=-1))
            link(nc.gpsimd.iota(tokn[:], pattern=[[P, T]], base=0, channel_multiplier=1,
                                allow_small_or_imprecise_dtypes=True))
            pool.wait_ge(sgw_in, 16)
            nc.gpsimd.affine_select(out=sgw_rows, in_=sgw_rows, compare_op=ALU.is_ge, fill=0.0, base=0,
                                    pattern=[[0, G], [-1, P]], channel_multiplier=1).then_inc(sgw_masked, 1)
            pool.wait_ge(rel_stored, 16)
            pool.wait_ge(wT_ready, 1)
            for h in range(H):
                if h >= 2:
                    pool.wait_ge(smax_ready, T * (h - 1))
                src = bass.AP(rel_rows.tensor, h * 5 * P, [[1, P], [1, 4 * P]])
                pool.dma_start(relM[:, h % 2, :], src).then_inc(relM_in, 16)
                pool.wait_ge(relM_in, 16 * (h + 1))
                nc.gpsimd.memset(relM[0:64, h % 2, 0:64], NEG).then_inc(relM_ready, 1)
            pool.wait_ge(unit_ready, A_BASE)
            link(nc.gpsimd.iota(iota_s, pattern=[[1, S]], base=0, channel_multiplier=0,
                                allow_small_or_imprecise_dtypes=True))
            pool.dma_start(g2, norm2_g[0:1, :].to_broadcast([P, D])).then_inc(late_in, 16)
            pool.dma_start(rw, router_w[0].rearrange("(k p) e -> p k e", p=P)).then_inc(late_in, 16)
            pool.wait_ge(unit_ready, O_BASE)
            for t in range(T):
                pool.dma_start(x2[:, t, :], x_rows[t * P:(t + 1) * P, :]).then_inc(x_again, 16)
            link(nc.gpsimd.memset(xg, 0.0))
            pool.wait_ge(unit_ready, UNITS)
            link(nc.gpsimd.iota(iota_e, pattern=[[1, E]], base=0, channel_multiplier=0,
                                allow_small_or_imprecise_dtypes=True))
            pool.dma_start(rb_all, router_b[0:1, :].to_broadcast([P, E])).then_inc(late_in, 16)
            pool.wait_ge(h2_stored, 16 * T)
            pool.wait_ge(out_stored, 16 * T)
            pool.wait_ge(routed, 1)

            def gather(n, item, first=False):
                def go(rows_):
                    nc.gpsimd.indirect_dma_start(
                        out=xg[0:rows_, :], out_offset=None, in_=h2_rows[:, :],
                        in_offset=bass.IndirectOffsetOnAxis(ap=plan_i[0:rows_, 0:1], axis=0)).then_inc(gathered, 16)
                pool.wait_ge(plan_ready, item + 1)
                if not first:
                    pool.wait_ge(xg_turned, item)
                settle(pool)
                by_rows(pool, n, go)

            def scatter(n, item, first=False):
                def go(rows_):
                    nc.gpsimd.indirect_dma_start(
                        out=out_rows[:, :], out_offset=bass.IndirectOffsetOnAxis(ap=plan_i[0:rows_, 1:2], axis=0),
                        in_=yrow[0:rows_, :], in_offset=None, compute_op=ALU.add).then_inc(scattered, 16)
                pool.wait_ge(y_ready, item + 1)
                if not first:
                    pool.wait_ge(scattered, item * 16)
                settle(pool)
                by_rows(pool, n, go)

            gather(load(pool, N_AT, S), 0, first=True)
            gather(load(pool, N_AT + 1, S), 1)
            scatter(load(pool, N_AT, S), 0, first=True)
            with pool.Fori(1, E) as i:
                n, nn = load(pool, i + N_AT, S), load(pool, i + (N_AT + 1), S)
                gather(nn, i + 1)
                scatter(n, i)
            n_extra = load(pool, NX_AT, EXTRA)
            with pool.Fori(0, EXTRA) as b:
                with pool.If(b < n_extra):
                    pool.wait_ge(plan_ready, b + (E + 2))
                    pool.wait_ge(xg_turned, b + (E + 1))
                    settle(pool)
                    nc.gpsimd.indirect_dma_start(
                        out=xg, out_offset=None, in_=h2_rows[:, :],
                        in_offset=bass.IndirectOffsetOnAxis(ap=plan_i[:, 0:1], axis=0)).then_inc(gathered, 16)
                    pool.wait_ge(y_ready, b + (E + 1))
                    pool.wait_ge(scattered, b * 16 + E * 16)
                    settle(pool)
                    nc.gpsimd.indirect_dma_start(
                        out=out_rows[:, :], out_offset=bass.IndirectOffsetOnAxis(ap=plan_i[:, 1:2], axis=0),
                        in_=yrow, in_offset=None, compute_op=ALU.add).then_inc(scattered, 16)
                with pool.Else():
                    pool.nop()
            pool.wait_ge(gathered, n_extra * 16 + (E + 1) * 16)
            pool.wait_ge(scattered, n_extra * 16 + E * 16)

        @block.scalar
        def _(act):
            made = [0]

            def link(ins):
                made[0] += 1
                ins.then_inc(act_chain, 1)
                act.wait_ge(act_chain, made[0])

            act.dma_start(rows[0:KD, :], norm1_g.rearrange("l (k p) -> (l k) p", p=P)).then_inc(rows_in, 16)
            for r, g in ((KD, q_norm_g), (KD + 1, k_norm_g)):
                for half in range(2):
                    act.dma_start(rows[r:r + 1, half * DH:(half + 1) * DH], g[0:1, :]).then_inc(rows_in, 16)
            act.dma_start(sgw_rows, sg_w[0].rearrange("g t s -> t g s")).then_inc(sgw_in, 16)
            act.dma_start(rel_in[0:H, :], rel_bias[0]).then_inc(rel_in_s, 16)
            act.dma_start(bias_rows[:, 0:4, :], b_gate_up.rearrange("l e (m p) -> (l e m) p", p=P)
                          .rearrange("(c r) p -> r c p", r=P)).then_inc(bias_in, 16)
            act.dma_start(bias_rows[:, 4:6, :], b_down.rearrange("l e (m p) -> (l e m) p", p=P)
                          .rearrange("(c r) p -> r c p", r=P)).then_inc(bias_in, 16)
            act.wait_ge(cols_ready, 1)
            for t in range(T):
                act.wait_ge(x_in[t], 16)
                if t:
                    act.wait_ge(x_sq, t)
                nc.scalar.activation(scratch, xin[:, t, :], ACT.Square,
                                     accum_out=stat[:, t:t + 1]).then_inc(x_sq, 1)
            act.wait_ge(x_sq, T)
            link(nc.scalar.activation(rstd[:, 0:T], stat[:, 0:T], ACT.Sqrt, bias=eps[:, 0:1], scale=1.0 / D))
            act.wait_ge(rel_ready, 1)
            act.dma_start(rel_rows[:, :], rel_out[0:H, :]).then_inc(rel_stored, 16)
            act.wait_ge(bias_turned, 1)
            nc.scalar.activation(biasT[:], TT[:, 0:768], ACT.Copy).then_inc(bias_ready, 1)
            act.wait_ge(sgw_turned, 1)
            act.wait_ge(ln_in, 48)
            nc.scalar.activation(wT, SBK[:, 1, :].rearrange("p (g n) -> p g n", g=G), ACT.Copy).then_inc(wT_ready, 1)
            for u in range(4):
                act.wait_ge(unit_ready, u + 1)
                if u:
                    act.wait_ge(qk_var, u)
                else:
                    act.wait_ge(xs_ready, T)
                nc.scalar.activation(scratch, PJ[:, u % 2, :], ACT.Square).then_inc(qk_sq, 1)
                act.wait_ge(qk_var, u + 1)
                if u:
                    act.wait_ge(unit_free[(u - 1) % 2], (u - 1) // 2 + 1)
                nc.scalar.activation(rstd[:, 0:16], stat[:, 0:16], ACT.Sqrt, bias=eps[:, 0:1],
                                     scale=1.0 / DH).then_inc(qk_std, 1)
            for u in (4, 5):
                act.wait_ge(unit_ready, u + 1)
                nc.scalar.activation(vv[:, :, (u - 4) * PAIRC:(u - 3) * PAIRC],
                                     PJ[:, u % 2, :].rearrange("p (t n) -> p t n", t=T),
                                     ACT.Copy).then_inc(unit_free[u % 2], 1)
            for u in (6, 7):
                act.wait_ge(unit_ready, u + 1)
                nc.scalar.activation(vn[:, :, (u - 6) * PAIRC:(u - 5) * PAIRC],
                                     PJ[:, u % 2, :].rearrange("p (t n) -> p t n", t=T),
                                     ACT.Gelu_apprx_tanh).then_inc(unit_free[u % 2], 1)
            for u in range(U_BASE, B_BASE):
                act.wait_ge(unit_ready, u + 1)
                nc.scalar.activation(uT[:, u - U_BASE, :], PJ[:, u % 2, 0:512],
                                     ACT.Gelu_apprx_tanh).then_inc(unit_free[u % 2], 1)
            for c in range(2):
                act.wait_ge(vc_ready, c + 1)
                if c:
                    act.wait_ge(v_var, c)
                nc.scalar.activation(scratch, vn[:, :, c * PAIRC:(c + 1) * PAIRC], ACT.Square).then_inc(vc_sq, 1)
                act.wait_ge(v_var, c + 1)
                nc.scalar.activation(rstd[:, 8 * c:8 * c + 8], stat[:, 8 * c:8 * c + 8], ACT.Sqrt, bias=eps[:, 0:1],
                                     scale=1.0 / P).then_inc(v_std, 1)

            def attend(s):
                if s < T * H:
                    a, n = s, (s % T + 1) * P
                    act.wait_ge(smax_ready, a + 1)
                    if a >= 2:
                        act.wait_ge(probs_turned, a - 1)
                    nc.scalar.activation(prow[:, a % 2, 0:n], srow[:, a % 2, 0:n], ACT.Exp,
                                         bias=nmax[:, a % 2:a % 2 + 1],
                                         accum_out=ssum[:, a % 2:a % 2 + 1]).then_inc(exp_ready, 1)
                if 2 <= s < T * H + 2:
                    a, n = s - 2, ((s - 2) % T + 1) * P
                    act.wait_ge(probs_turned, a + 1)
                    if a >= 2:
                        act.wait_ge(pv_done, a - 1)
                    nc.scalar.activation(pcol[:, a % 2, 0:n], PT[:, 0:n], ACT.Copy).then_inc(pcol_ready, 1)
                if s >= 3 and (s - 3) % 8 == 7:
                    hp = (s - 3) // 8
                    act.wait_ge(pv_done, 8 * (hp + 1))
                    nc.scalar.activation(qT[:, hp, :], PV, ACT.Copy).then_inc(attn_ready, 1)

            def open_gate(u):
                n = u - B_BASE
                act.wait_ge(unit_ready, u + 1)
                if n >= 2:
                    act.wait_ge(merged_ready, n - 1)
                nc.scalar.activation(gate[:, n % 2, :], PJ[:, u % 2, 0:512], ACT.Sigmoid).then_inc(gate_ready, 1)

            act.wait_ge(vn_ready, 2)
            for s in range(T * H + 3):
                attend(s)
                if s < T * H and s % 4 == 3:
                    open_gate(B_BASE + s // 4)
            for m in range(KD):
                open_gate(A_BASE + m)
            act.wait_ge(merged_ready, 2 * KD)
            act.wait_ge(x2_ready, 4)
            for t in range(T):
                if t:
                    act.wait_ge(x2_sq, t)
                nc.scalar.activation(scratch, x2[:, t, :], ACT.Square, accum_out=stat[:, t:t + 1]).then_inc(x2_sq, 1)
            act.wait_ge(x2_sq, T)
            nc.scalar.activation(rstd[:, 0:T], stat[:, 0:T], ACT.Sqrt, bias=eps[:, 0:1],
                                 scale=1.0 / D).then_inc(x2_std, 1)
            for t in range(T):
                act.wait_ge(h2_turned, t + 1)
                nc.scalar.activation(h2T[:, :, t * P:(t + 1) * P],
                                     PJ[:, t % 2, :].rearrange("p (k n) -> p k n", k=KD), ACT.Copy).then_inc(h2T_ready, 1)
            for t in range(T):
                act.wait_ge(top_ready, 1)
                nc.scalar.activation(prob[:, t, :], top[:, t, 0:TOPK], ACT.Exp, bias=neg_t[:, t:t + 1],
                                     accum_out=psum_t[:, t:t + 1]).then_inc(top_exp, 1)
            act.wait_ge(routed, 1)

            def turned_in(item):
                act.wait_ge(xg_turned, item + 1)
                nc.scalar.activation(xT, TT[:, :].rearrange("p (k n) -> p k n", k=KD), ACT.Copy).then_inc(xT_ready, 1)

            def sigmoids(item):
                def go(n):
                    for half in range(2):
                        ms = slice(4 * half, 4 * half + 4)
                        act.wait_ge(g_ready, item * 2 + (half + 1))
                        nc.scalar.activation(es[:, ms, 0:n], eg[:, ms, 0:n], ACT.Sigmoid,
                                             scale=ALPHA).then_inc(s_ready, 1)
                return go

            def results(item, first=False):
                def go(n):
                    act.wait_ge(y_turned, item + 1)
                    if not first:
                        act.wait_ge(scattered, item * 16)
                    nc.scalar.activation(yrow[0:n, :], TT[0:n, :], ACT.Copy,
                                         scale=plan_w[0:n, 1:2]).then_inc(y_ready, 1)
                return go

            turned_in(0)
            n0 = load(act, N_AT, S)
            by_rows(act, n0, sigmoids(0))
            turned_in(1)
            by_rows(act, n0, results(0, first=True))
            with act.Fori(1, E) as i:
                n = load(act, i + N_AT, S)
                by_rows(act, n, sigmoids(i))
                turned_in(i + 1)
                by_rows(act, n, results(i))
            n_extra = load(act, NX_AT, EXTRA)
            with act.Fori(0, EXTRA) as b:
                with act.If(b < n_extra):
                    turned_in(b + (E + 1))
                    sigmoids(b + E)(P)
                    results(b + E)(P)
                with act.Else():
                    act.nop()

        @block.vector
        def _(dve):
            made = [0]

            def link(ins):
                made[0] += 1
                ins.then_inc(dve_chain, 1)
                dve.wait_ge(dve_chain, made[0])

            def t_major(ap):
                return ap.rearrange("p (t n) -> p t n", t=T)

            link(nc.vector.memset(eps[:], EPS))
            dve.wait_ge(cols_turned, 1)
            nc.vector.tensor_copy(colT[:], SBK[:, 0, 0:10]).then_inc(cols_ready, 1)
            dve.wait_ge(rel_in_s, 16)
            own = CLIP + P
            link(nc.vector.tensor_copy(rel_out[0:H, 0:own], rel_in[0:H, REL - own:REL]))
            nc.vector.tensor_copy(rel_out[0:H, own:5 * P],
                                  rel_in[0:H, REL - 1:REL].to_broadcast([H, 5 * P - own])).then_inc(rel_ready, 1)
            dve.wait_ge(act_chain, 1)
            link(nc.vector.reciprocal(rstd[:, 0:T], rstd[:, 0:T]))
            for t in range(T):
                nc.vector.tensor_scalar(xin[:, t, :], xin[:, t, :], rstd[:, t:t + 1], None, ALU.mult).then_inc(xs_ready, 1)
            dve.wait_ge(cols_ready, 1)
            for t in range(T):
                dve.wait_ge(x_turned, t + 1)
                nc.vector.tensor_tensor(hT[:, :, t * P:(t + 1) * P],
                                        PJ[:, t % 2, :].rearrange("p (k n) -> p k n", k=KD),
                                        colT[:, 0:KD].unsqueeze(2).to_broadcast([P, KD, P]),
                                        ALU.mult).then_inc(hT_ready, 1)

            def turned_qk(n):
                dve.wait_ge(qk_turned, n + 1)
                is_k, hp = divmod(n, HP)
                nc.vector.tensor_scalar((kT if is_k else qT)[:, hp, :], SBK[:, n % 2, :],
                                        colT[:, KD + is_k:KD + is_k + 1],
                                        1.0 if is_k else float(DH) ** -0.5, ALU.mult, ALU.mult).then_inc(qk_ready, 1)

            for u in range(4):
                dve.wait_ge(qk_sq, u + 1)
                if u:
                    dve.wait_ge(qk_std, u)
                nc.vector.tensor_reduce(stat[:, 0:16], scratch.rearrange("p (a n) -> p a n", n=DH),
                                        AX_X, ALU.add).then_inc(qk_var, 1)
                dve.wait_ge(qk_std, u + 1)
                link(nc.vector.reciprocal(rstd[:, 0:16], rstd[:, 0:16]))
                dst = qk_rows[u // 2][:, :, (u % 2) * PAIRC:(u % 2 + 1) * PAIRC]
                nc.vector.tensor_tensor(dst.rearrange("p t (h n) -> p t h n", n=DH),
                                        PJ[:, u % 2, :].rearrange("p (t h n) -> p t h n", t=T, n=DH),
                                        rstd[:, 0:16].rearrange("p (t h) -> p t h", t=T).unsqueeze(3)
                                        .to_broadcast([P, T, 4, DH]), ALU.mult).then_inc(unit_free[u % 2], 1)
            for n in range(2 * HP):
                turned_qk(n)
            for c in range(2):
                u = 6 + c
                dve.wait_ge(unit_free[u % 2], u // 2 + 1)
                part = vn[:, :, c * PAIRC:(c + 1) * PAIRC].rearrange("p t (g n) -> p t g n", n=P)
                bc = [P, T, 2, P]
                if c:
                    dve.wait_ge(v_std, c)
                link(nc.vector.tensor_reduce(mean[:, 0:8].rearrange("p (t g) -> p t g", t=T), part, AX_X, ALU.add))
                link(nc.vector.tensor_scalar(mean[:, 0:8], mean[:, 0:8], 1.0 / P, None, ALU.mult))
                nc.vector.tensor_tensor(part, part, mean[:, 0:8].rearrange("p (t g) -> p t g", t=T).unsqueeze(3)
                                        .to_broadcast(bc), ALU.subtract).then_inc(vc_ready, 1)
                dve.wait_ge(vc_sq, c + 1)
                nc.vector.tensor_reduce(stat[:, 8 * c:8 * c + 8], scratch.rearrange("p (a n) -> p a n", n=P),
                                        AX_X, ALU.add).then_inc(v_var, 1)
                dve.wait_ge(v_std, c + 1)
                link(nc.vector.reciprocal(rstd[:, 8 * c:8 * c + 8], rstd[:, 8 * c:8 * c + 8]))
                link(nc.vector.tensor_tensor(part, part, rstd[:, 8 * c:8 * c + 8].rearrange("p (t g) -> p t g", t=T)
                                             .unsqueeze(3).to_broadcast(bc), ALU.mult))
                cols = slice(c * PAIRC, (c + 1) * PAIRC)
                link(nc.vector.tensor_tensor(vn[:, :, cols], vn[:, :, cols],
                                             ln_g[:, cols].unsqueeze(1).to_broadcast([P, T, PAIRC]), ALU.mult))
                nc.vector.tensor_tensor(vn[:, :, cols], vn[:, :, cols],
                                        ln_b[:, cols].unsqueeze(1).to_broadcast([P, T, PAIRC]),
                                        ALU.add).then_inc(vn_ready, 1)
            for g in range(G):
                u = U_BASE + g
                dve.wait_ge(mixed, g + 1)
                dve.wait_ge(unit_free[u % 2], u // 2 + 1)
                if g:
                    dve.wait_ge(sgu_ready, g)
                link(nc.vector.tensor_tensor(gated.rearrange("p (n t) -> p n t", t=P),
                                             SBK[:, g % 2, :].rearrange("p (n t) -> p n t", t=P),
                                             sgb[:, g, :].unsqueeze(1).to_broadcast([P, T, P]), ALU.add))
                nc.vector.tensor_tensor(uT[:, g, :], gated, uT[:, g, :], ALU.mult).then_inc(sgu_ready, 1)

            dve.wait_ge(sgu_ready, G)

            def attend(s):
                if s < T * H:
                    h, t = divmod(s, T)
                    n = (t + 1) * P
                    dve.wait_ge(scores_ready, s + 1)
                    dve.wait_ge(relM_ready, h + 1)
                    if s >= 2:
                        dve.wait_ge(exp_ready, s - 1)
                    nc_max = nc.vector.tensor_tensor_reduce(
                        srow[:, s % 2, 0:n], SBK[:, s % 2, 0:n], relM[:, h % 2, 0:n][:, ::-1], 1.0, -3e38,
                        ALU.add, ALU.max, smax[:, s % 2:s % 2 + 1])
                    link(nc_max)
                    nc.vector.tensor_scalar(nmax[:, s % 2:s % 2 + 1], smax[:, s % 2:s % 2 + 1], -1.0, None,
                                            ALU.mult).then_inc(smax_ready, 1)
                if 1 <= s <= T * H:
                    a, n = s - 1, ((s - 1) % T + 1) * P
                    dve.wait_ge(exp_ready, a + 1)
                    link(nc.vector.reciprocal(rsum[:, a % 2:a % 2 + 1], ssum[:, a % 2:a % 2 + 1]))
                    nc.vector.tensor_scalar(prow[:, a % 2, 0:n], prow[:, a % 2, 0:n], rsum[:, a % 2:a % 2 + 1], None,
                                            ALU.mult).then_inc(probs_ready, 1)

            def merge(u):
                n, m = u - B_BASE, (u - B_BASE) % KD
                dve.wait_ge(gate_ready, n + 1)
                if n < KD:
                    nc.vector.tensor_tensor(merged[:, m, :], gate[:, n % 2, :], PJ[:, u % 2, 512:1024],
                                            ALU.mult).then_inc(unit_free[u % 2], 1)
                    dve.wait_ge(unit_free[u % 2], u // 2 + 1)
                    nc.vector.engine_nop().then_inc(merged_ready, 1)
                else:
                    dve.wait_ge(merged_ready, n)
                    nc.vector.tensor_tensor(gated, gate[:, n % 2, :], PJ[:, u % 2, 512:1024],
                                            ALU.mult).then_inc(unit_free[u % 2], 1)
                    dve.wait_ge(unit_free[u % 2], u // 2 + 1)
                    nc.vector.tensor_tensor(merged[:, m, :], merged[:, m, :], gated, ALU.add).then_inc(merged_ready, 1)

            for s in range(T * H + 1):
                attend(s)
                if s < T * H and s % 4 == 3:
                    merge(B_BASE + s // 4)
            for m in range(KD):
                merge(A_BASE + m)
            dve.wait_ge(x_again, 16 * T)
            for c in range(4):
                u = O_BASE + c
                dve.wait_ge(unit_ready, u + 1)
                part = x2[:, :, c * PAIRC:(c + 1) * PAIRC]
                nc.vector.tensor_tensor(part, part, t_major(PJ[:, u % 2, :]), ALU.add).then_inc(x2_ready, 1)
            dve.wait_ge(x2_std, 1)
            link(nc.vector.reciprocal(rstd[:, 0:T], rstd[:, 0:T]))
            dve.wait_ge(late_in, 48)
            for t in range(T):
                nc.vector.scalar_tensor_tensor(h2[:, t, :], x2[:, t, :], rstd[:, t:t + 1], g2, ALU.mult,
                                               ALU.mult).then_inc(h2_ready, 1)
            bc = [P, T, E]
            dve.wait_ge(logits_ready, 1)
            link(nc.vector.tensor_tensor(logits, SBK[:, 0, 0:TE].rearrange("p (t e) -> p t e", t=T),
                                         rb_all.unsqueeze(1).to_broadcast(bc), ALU.add))
            for t in range(T):
                link(nc.vector.max(top[:, t, :], logits[:, t, :]))
                link(nc.vector.max_index(top_i[:, t, :], top[:, t, :], logits[:, t, :]))
            link(nc.vector.tensor_scalar(neg_t, top[:, :, 0], -1.0, None, ALU.mult))
            nc.vector.tensor_copy(top_f, top_i).then_inc(top_ready, 1)
            dve.wait_ge(top_ready, 1)
            dve.wait_ge(pool_made, 9 - 1)
            for k in range(TOPK):
                idx = top_f[:, :, k:k + 1].to_broadcast(bc)
                ie = iota_e.unsqueeze(1).to_broadcast(bc)
                if k == 0:
                    link(nc.vector.tensor_tensor(chosen, ie, idx, ALU.is_equal))
                else:
                    link(nc.vector.tensor_tensor(hit, ie, idx, ALU.is_equal))
                    link(nc.vector.tensor_tensor(chosen, chosen, hit, ALU.add))
            nc.vector.engine_nop().then_inc(chosen_ready, 1)
            dve.wait_ge(top_exp, T)
            link(nc.vector.reciprocal(psum_t, psum_t))
            link(nc.vector.tensor_tensor(prob, prob, psum_t.unsqueeze(2).to_broadcast([P, T, TOPK]), ALU.mult))
            for k in range(TOPK):
                idx = top_f[:, :, k:k + 1].to_broadcast(bc)
                pk = prob[:, :, k:k + 1].to_broadcast(bc)
                link(nc.vector.tensor_tensor(hit, ie, idx, ALU.is_equal))
                if k == 0:
                    link(nc.vector.tensor_tensor(weight, hit, pk, ALU.mult))
                else:
                    link(nc.vector.tensor_tensor(hit, hit, pk, ALU.mult))
                    link(nc.vector.tensor_tensor(weight, weight, hit, ALU.add))
            link(nc.vector.tensor_copy(vals[:, :, 0:E, 1], weight))
            link(nc.vector.tensor_copy(vals[:, :, E, 1], weight[:, :, E - 1]))
            link(nc.vector.tensor_copy(vals[:, :, :, 0], tokn[:].unsqueeze(2).to_broadcast([P, T, E + 1])))
            dve.wait_ge(counted, 1)
            link(nc.vector.tensor_copy(before, SBK[:, 1, 0:TE].rearrange("p (t e) -> p t e", t=T)))
            link(nc.vector.tensor_tensor(place_a, tokn[:].unsqueeze(2).to_broadcast(bc), before, ALU.subtract))
            link(nc.vector.tensor_tensor(place_a, place_a,
                                         SBK[:, 1, TE:TE + E].unsqueeze(1).to_broadcast(bc), ALU.add))
            link(nc.vector.tensor_tensor(before, before, place_a, ALU.subtract))
            link(nc.vector.tensor_tensor(before, before, chosen, ALU.mult))
            link(nc.vector.tensor_tensor(pos[:, :, 0:E], before, place_a, ALU.add))
            link(nc.vector.tensor_copy(pos[:, :, E:E + 1], pos[:, :, E - 1:E]))
            link(nc.vector.tensor_copy(table[0:1, 0:E], SBK[0:1, 1, TE:TE + E]))
            link(nc.vector.tensor_copy(table[0:1, E:E + 1], SBK[0:1, 1, TE + E - 1:TE + E]))
            link(nc.vector.tensor_copy(col_cnt, SBK[0:E, 1, TE + E:TE + E + 1]))
            for b in range(3):
                link(nc.vector.tensor_scalar(col_fl[:, b:b + 1], col_cnt, float((b + 1) * P), None, ALU.is_gt))
            link(nc.vector.tensor_reduce(col_nb, col_fl, AX_X, ALU.add))
            link(nc.vector.memset(col_eb[:, 0:2], 0.0))
            nc.vector.tensor_copy(col_eb[:, 0:1], tokn[0:E, 0:1]).then_inc(extra_cols, 1)
            dve.wait_ge(extra_base, 1)
            link(nc.vector.tensor_copy(col_base, SBK[0:E, 0, 0:1]))
            for b in range(3):
                link(nc.vector.tensor_scalar(col_code, col_base, float(b), None, ALU.add))
                link(nc.vector.tensor_scalar(oh_x[:, b, :], iota_e[0:E, 0:EXTRA + 1], col_code, col_fl[:, b:b + 1],
                                             ALU.is_equal, ALU.mult))
            link(nc.vector.memset(col_eb[:, 1:2], 1.0))
            nc.vector.engine_nop().then_inc(extra_hot, 1)
            dve.wait_ge(extra_ready, 1)
            J = EXTRA + 1
            link(nc.vector.tensor_copy(table[0:1, XE_AT:XE_AT + J], SBK[0:1, 0, 16:16 + J]))
            link(nc.vector.tensor_copy(table[0:1, XB_AT:XB_AT + J], SBK[0:1, 0, 32:32 + J]))
            nc.vector.tensor_copy(table[0:1, NX_AT:NX_AT + 1], SBK[0:1, 0, 48:49]).then_inc(routed, 1)
            dve.wait_ge(routed, 1)
            BASE = made[0]

            def plan(e, slots, item, base, at):
                for t in range(T):
                    dve_i = nc.vector.tensor_scalar(onehot[:, t, :], slots, pos[:, t, bass.ds(e, 1)], None, ALU.is_equal)
                    dve_i.then_inc(hot_ready, 1)
                nc.vector.tensor_copy(val_e[:, :, :], vals[:, :, bass.ds(e, 1), :].rearrange("p t o c -> p t (o c)")) \
                    .then_inc(hot_ready, 1)
                dve.wait_ge(plan_there, item + 1)
                nc.vector.tensor_copy(plan_w[:, 0:1], YD[:, 1:2]).then_inc(dve_chain, 1)
                dve.wait_ge(dve_chain, base + at + 1)
                nc.vector.tensor_copy(plan_i[:, 0:1], YD[:, 0:1]).then_inc(plan_ready, 1)

            def take_plan(item, base, at, first=False):
                dve.wait_ge(plan_ready, item + 1)
                if not first:
                    dve.wait_ge(scattered, item * 16)
                nc.vector.tensor_copy(plan_w[:, 1:2], plan_w[:, 0:1]).then_inc(dve_chain, 1)
                nc.vector.tensor_copy(plan_i[:, 1:2], plan_i[:, 0:1]).then_inc(dve_chain, 1)
                dve.wait_ge(dve_chain, base + at + 2)

            def finish(e, item, base, at):
                def go(n):
                    c = at

                    def link_(ins):
                        nonlocal c
                        c += 1
                        ins.then_inc(dve_chain, 1)
                        dve.wait_ge(dve_chain, base + c)

                    for half in range(2):
                        ms = slice(4 * half, 4 * half + 4)
                        g_ps = PJ[:, 0, 512 * half:512 * half + 512].rearrange("p (m n) -> p m n", m=4)[:, :, 0:n]
                        u_ps = PJ[:, 1, 512 * half:512 * half + 512].rearrange("p (m n) -> p m n", m=4)[:, :, 0:n]
                        bg = bguT[:, bass.ds(e * (2 * FT) + 4 * half, 4)].unsqueeze(2).to_broadcast([P, 4, n])
                        bu = bguT[:, bass.ds(e * (2 * FT) + (FT + 4 * half), 4)].unsqueeze(2).to_broadcast([P, 4, n])
                        dve.wait_ge(gu_ready, item * 2 + (half + 1))
                        link_(nc.vector.tensor_tensor(eg[:, ms, 0:n], g_ps, bg, ALU.add))
                        nc.vector.tensor_scalar(eg[:, ms, 0:n], eg[:, ms, 0:n], LIMIT, None, ALU.min).then_inc(g_ready, 1)
                        link_(nc.vector.tensor_tensor(eu[:, ms, 0:n], u_ps, bu, ALU.add))
                        link_(nc.vector.tensor_scalar(eu[:, ms, 0:n], eu[:, ms, 0:n], LIMIT, -LIMIT, ALU.min, ALU.max))
                        dve.wait_ge(g_ready, item * 2 + (half + 1))
                        link_(nc.vector.scalar_tensor_tensor(eu[:, ms, 0:n], eu[:, ms, 0:n], 1.0, eg[:, ms, 0:n],
                                                             ALU.add, ALU.mult))
                        dve.wait_ge(s_ready, item * 2 + (half + 1))
                        nc.vector.tensor_tensor(hh[:, ms, 0:n], eu[:, ms, 0:n], es[:, ms, 0:n], ALU.mult).then_inc(hh_ready, 1)
                    for half in range(2):
                        ms = slice(4 * half, 4 * half + 4)
                        y_ps = YD[:, 512 * half:512 * half + 512].rearrange("p (m n) -> p m n", m=4)[:, :, 0:n]
                        bd = bdT[:, bass.ds(e * KD + 4 * half, 4)].unsqueeze(2).to_broadcast([P, 4, n])
                        dve.wait_ge(yd_ready, item * 2 + (half + 1))
                        nc.vector.tensor_tensor(yT[:, ms, 0:n], y_ps, bd, ALU.add).then_inc(yT_ready, 1)
                    assert c - at == 8
                return go

            first_slots = iota_s[:, 0:P]
            plan(0, first_slots, 0, BASE, 0)
            take_plan(0, BASE, 1, first=True)
            dve.wait_ge(gathered, 16)
            plan(1, first_slots, 1, BASE, 3)
            by_rows(dve, load(dve, N_AT, S), finish(0, 0, BASE, 4))
            B1, STEP = BASE + 12, 11
            with dve.Fori(1, E) as i:
                base = i * STEP + (B1 - STEP)
                take_plan(i, base, 0)
                dve.wait_ge(gathered, i * 16 + 16)
                plan(i + 1, first_slots, i + 1, base, 2)
                by_rows(dve, load(dve, i + N_AT, S), finish(i, i, base, 3))
            B2 = B1 + (E - 1) * STEP
            n_extra = load(dve, NX_AT, EXTRA)
            with dve.Fori(0, EXTRA) as b:
                with dve.If(b < n_extra):
                    e = load(dve, b + XE_AT, E - 1)
                    nb = load(dve, b + XB_AT, 3)
                    base = b * STEP + B2
                    dve.wait_ge(scattered, b * 16 + E * 16)
                    dve.wait_ge(gathered, b * 16 + (E + 1) * 16)
                    plan(e, iota_s[:, bass.ds(nb * P, P)], b + (E + 1), base, 0)
                    dve.wait_ge(plan_ready, b + (E + 2))
                    nc.vector.tensor_copy(plan_w[:, 1:2], plan_w[:, 0:1]).then_inc(dve_chain, 1)
                    nc.vector.tensor_copy(plan_i[:, 1:2], plan_i[:, 0:1]).then_inc(dve_chain, 1)
                    dve.wait_ge(dve_chain, base + 3)
                    finish(e, b + E, base, 3)(P)
                with dve.Else():
                    dve.nop()

        @block.tensor
        def _(pe):
            mm = nc.tensor.matmul

            def have(c):
                pe.wait_ge(arrived[slot(c)], 16 * uses(c))

            def wchunk(c, n):
                return ring[:, slot(c), :].rearrange("p (k n) -> p k n", n=n)

            pe.wait_ge(pool_made, 5)
            pe.wait_ge(rows_in, 16 * 5)
            nc.tensor.transpose(SBK[:, 0, 0:KD + 2], rows[0:KD + 2, :], ident[0:KD + 2, 0:KD + 2]).then_inc(cols_turned, 1)
            pe.wait_ge(bias_in, 32)
            for c in range(6):
                last = nc.tensor.transpose(TT[:, c * P:(c + 1) * P], bias_rows[:, c, :], ident[:])
            last.then_inc(bias_turned, 1)
            pe.wait_ge(sgw_masked, 1)
            for g in range(G):
                last = nc.tensor.transpose(SBK[:, 1, g * P:(g + 1) * P], sgw_rows[:, g, :], ident[:])
            last.then_inc(sgw_turned, 1)
            for t in range(T):
                pe.wait_ge(xs_ready, t + 1)
                if t >= 2:
                    pe.wait_ge(hT_ready, t - 1)
                for k in range(KD):
                    last = nc.tensor.transpose(PJ[:, t % 2, k * P:(k + 1) * P], xin[:, t, k * P:(k + 1) * P], ident[:])
                last.then_inc(x_turned, 1)
            pe.wait_ge(hT_ready, T)

            def start_unit(u):
                have(UNIT_CHUNK[u])
                if u >= 2:
                    pe.wait_ge(unit_free[u % 2], free_before(u))

            def by_tokens(u, lhs):
                if u < O_BASE + 2:
                    start_unit(u)
                else:
                    have(UNIT_CHUNK[u])
                    pe.wait_ge(x2_ready, u - O_BASE - 1)
                w = wchunk(UNIT_CHUNK[u], PAIRC)
                for t in range(T):
                    for k in range(KD):
                        last = mm(PJ[:, u % 2, t * PAIRC:(t + 1) * PAIRC], lhs[:, k, t * P:(t + 1) * P], w[:, k, :],
                                  start=(k == 0), stop=(k == KD - 1))
                last.then_inc(unit_ready, 1)

            def turn_qk(n):
                is_k, hp = divmod(n, HP)
                if n >= 2:
                    pe.wait_ge(qk_ready, n - 1)
                for t in range(T):
                    last = nc.tensor.transpose(SBK[:, n % 2, t * P:(t + 1) * P],
                                               qk_rows[is_k][:, t, hp * P:(hp + 1) * P], ident[:])
                last.then_inc(qk_turned, 1)

            for u in range(8):
                by_tokens(u, hT)
                if u == 5:
                    pe.wait_ge(unit_free[1], 2)
                    pe.wait_ge(unit_free[0], 2)
                    pe.wait_ge(cols_ready, 1)
                    pe.wait_ge(wT_ready, 1)
                    for n in range(2 * HP):
                        turn_qk(n)

            def by_features(u, m, ks):
                w = wchunk(UNIT_CHUNK[u], PAIRC)
                for k in ks:
                    last = mm(PJ[:, u % 2, 0:512], w[:, k, (m % 2) * P:(m % 2 + 1) * P], hT[:, k, :],
                              start=(k == 0), stop=(k == KD - 1))
                return last

            def branch(u, kind, m, ks, lhs):
                c = BRANCH_CHUNK[(kind, m // 4)]
                have(c)
                w = wchunk(c, 512)
                for k in ks:
                    last = mm(PJ[:, u % 2, 512:1024], w[:, k, (m % 4) * P:(m % 4 + 1) * P], lhs[:, k, :],
                              start=(k == 0), stop=(k == 3))
                return last

            for m in range(4):
                u = U_BASE + m
                start_unit(u)
                by_features(u, m, range(KD)).then_inc(unit_ready, 1)
            pe.wait_ge(vn_ready, 2)
            pe.wait_ge(qk_ready, 2 * HP)
            for g in range(G):
                if g >= 2:
                    pe.wait_ge(sgu_ready, g - 1)
                for n in range(T):
                    last = mm(SBK[:, g % 2, n * P:(n + 1) * P], vn[:, n, g * P:(g + 1) * P], wT[:, g, :],
                              start=True, stop=True)
                last.then_inc(mixed, 1)

            def attend(s):
                if s < T * H:
                    h, t = divmod(s, T)
                    rows_ = slice(64 * (h % 2), 64 * (h % 2) + 64)
                    if s >= 2:
                        pe.wait_ge(smax_ready, s - 1)
                    mm(SBK[:, s % 2, 0:(t + 1) * P], qT[rows_, h // 2, t * P:(t + 1) * P], kT[rows_, h // 2, 0:(t + 1) * P],
                       start=True, stop=True).then_inc(scores_ready, 1)
                if 2 <= s < T * H + 2:
                    a = s - 2
                    pe.wait_ge(probs_ready, a + 1)
                    if a:
                        pe.wait_ge(pcol_ready, a)
                    else:
                        pe.wait_ge(bias_ready, 1)
                    for kt in range(a % T + 1):
                        last = nc.tensor.transpose(PT[:, kt * P:(kt + 1) * P], prow[:, a % 2, kt * P:(kt + 1) * P], ident[:])
                    last.then_inc(probs_turned, 1)
                if s >= 3:
                    a = s - 3
                    h, t = divmod(a, T)
                    pe.wait_ge(pcol_ready, a + 1)
                    if a % 8 == 0 and a:
                        pe.wait_ge(attn_ready, a // 8)
                    for kt in range(t + 1):
                        last = mm(PV[64 * (h % 2):64 * (h % 2) + 64, t * P:(t + 1) * P],
                                  vv[:, kt, h * DH:(h + 1) * DH], pcol[:, a % 2, kt * P:(kt + 1) * P],
                                  start=(kt == 0), stop=(kt == t))
                    last.then_inc(pv_done, 1)

            pe.wait_ge(sgu_ready, G)
            pe.wait_ge(unit_free[1], 3)
            pe.wait_ge(unit_free[0], 3)
            for m in range(KD):
                u = B_BASE + m
                start_unit(u)
                by_features(u, m, range(0, 3))
                attend(4 * m)
                by_features(u, m, range(3, 6))
                attend(4 * m + 1)
                by_features(u, m, range(6, 8))
                branch(u, "b", m, range(0, 1), uT)
                attend(4 * m + 2)
                branch(u, "b", m, range(1, 4), uT).then_inc(unit_ready, 1)
                attend(4 * m + 3)
            for m in range(KD):
                u = A_BASE + m
                start_unit(u)
                if m == 0:
                    for s in range(3):
                        by_features(u, m, range(3 * s, min(3 * s + 3, KD)))
                        attend(T * H + s)
                    pe.wait_ge(attn_ready, HP)
                else:
                    by_features(u, m, range(KD))
                branch(u, "a", m, range(4), qT).then_inc(unit_ready, 1)
            pe.wait_ge(merged_ready, 2 * KD)
            for c in range(4):
                by_tokens(O_BASE + c, merged)
            pe.wait_ge(x2_ready, 4)
            for t in range(T):
                pe.wait_ge(h2_ready, t + 1)
                if t >= 2:
                    pe.wait_ge(h2T_ready, t - 1)
                for k in range(KD):
                    last = nc.tensor.transpose(PJ[:, t % 2, k * P:(k + 1) * P], h2[:, t, k * P:(k + 1) * P], ident[:])
                last.then_inc(h2_turned, 1)
            pe.wait_ge(late_in, 48)
            for t in range(T):
                pe.wait_ge(h2T_ready, t + 1)
                for k in range(KD):
                    last = mm(SBK[:, 0, t * E:(t + 1) * E], h2T[:, k, t * P:(t + 1) * P], rw[:, k, :],
                              start=(k == 0), stop=(k == KD - 1))
            last.then_inc(logits_ready, 1)
            pe.wait_ge(chosen_ready, 1)
            for t in range(T):
                for s in range(t + 1):
                    mm(SBK[:, 1, t * E:(t + 1) * E], before_m[:] if s == t else ones[:], chosen[:, s, :],
                       start=(s == 0), stop=(s == t))
            for t in range(T):
                mm(SBK[:, 1, TE:TE + E], ones[:], chosen[:, t, :], start=(t == 0), stop=(t == T - 1))
            for t in range(T):
                last = mm(SBK[0:E, 1, TE + E:TE + E + 1], chosen[:, t, :], ones[:, 0:1], start=(t == 0), stop=(t == T - 1))
            last.then_inc(counted, 1)
            pe.wait_ge(extra_cols, 1)
            mm(SBK[0:E, 0, 0:1], before_m[0:E, 0:E], col_nb, start=True, stop=True).then_inc(extra_base, 1)
            pe.wait_ge(extra_hot, 1)
            J = EXTRA + 1
            for b in range(3):
                mm(SBK[0:1, 0, 16:16 + J], col_eb[:, 0:1], oh_x[:, b, :], start=(b == 0), stop=(b == 2))
            for b in range(3):
                for again in range(b + 1):
                    mm(SBK[0:1, 0, 32:32 + J], col_eb[:, 1:2], oh_x[:, b, :], start=(b == 0), stop=(b == 2 and again == b))
            mm(SBK[0:1, 0, 48:49], col_eb[:, 1:2], col_nb, start=True, stop=True).then_inc(extra_ready, 1)
            pe.wait_ge(routed, 1)

            def plan(item):
                pe.wait_ge(hot_ready, item * (T + 1) + (T + 1))
                for t in range(T):
                    last = mm(YD[:, 0:2], onehot[:, t, :], val_e[:, t, :], start=(t == 0), stop=(t == T - 1))
                last.then_inc(plan_there, 1)

            def turn_in(item):
                pe.wait_ge(gathered, item * 16 + 16)
                for k in range(KD):
                    last = nc.tensor.transpose(TT[:, k * P:(k + 1) * P], xg[:, k * P:(k + 1) * P], ident[:])
                last.then_inc(xg_turned, 1)

            def arrived_in(j, item):
                pe.wait_ge(arrived[j], item * 16 + 16 * (SLOT_USES[j] + 1))

            def up(item, j, n):
                arrived_in(j, item)
                order = [(w, m) for half in range(2) for w in range(2) for m in range(4 * half, 4 * half + 4)]
                for w, m in order:
                    last = mm(PJ[:, w, m * P:m * P + n], ring[:, j, (w * FT + m) * P:(w * FT + m + 1) * P], xT[:, j, 0:n],
                              start=(j == 0 and m % 4 == 0), stop=(j == KD - 1), skip_group_check=True)
                    if j == KD - 1 and w == 1 and m == 3:
                        last.then_inc(gu_ready, 1)
                if j == KD - 1:
                    last.then_inc(gu_ready, 1)
                else:
                    last.then_inc(chunk_used, 1)

            def first_up(item):
                def go(n):
                    pe.wait_ge(xT_ready, item + 1)
                    up(item, 0, n)
                return go

            def rest_up(item):
                def go(n):
                    for j in range(1, KD):
                        up(item, j, n)
                return go

            def down(item):
                def go(n):
                    for j in range(KD, SLOTS):
                        arrived_in(j, item)
                        if j % 2 == 0:
                            pe.wait_ge(hh_ready, item * 2 + (1 + (j - KD) // 2))
                        f = 2 * (j - KD)
                        for m in range(KD):
                            for c in range(2):
                                last = mm(YD[:, m * P:m * P + n],
                                          ring[:, j, c * D + m * P:c * D + (m + 1) * P], hh[:, f + c, 0:n],
                                          start=(f + c == 0 and m % 4 == 0), stop=(f + c == FT - 1),
                                          skip_group_check=True)
                            if j == SLOTS - 1 and m % 4 == 3:
                                last.then_inc(yd_ready, 1)
                        if j < SLOTS - 1:
                            last.then_inc(chunk_used, 1)
                    for m in range(KD):
                        if m % 4 == 0:
                            pe.wait_ge(yT_ready, item * 2 + (1 + m // 4))
                            settle(pe)
                        last = nc.tensor.transpose(TT[0:n, m * P:(m + 1) * P], yT[:, m, 0:n], ident[:])
                    last.then_inc(y_turned, 1)
                return go

            plan(0)
            turn_in(0)
            n0 = load(pe, N_AT, S)
            by_rows(pe, n0, first_up(0))
            plan(1)
            by_rows(pe, n0, rest_up(0))
            turn_in(1)
            pe.wait_ge(xT_ready, 2)
            by_rows(pe, n0, down(0))
            with pe.Fori(1, E) as i:
                n = load(pe, i + N_AT, S)
                by_rows(pe, n, first_up(i))
                plan(i + 1)
                by_rows(pe, n, rest_up(i))
                pe.wait_ge(y_ready, i)
                turn_in(i + 1)
                pe.wait_ge(xT_ready, i + 2)
                by_rows(pe, n, down(i))
            n_extra = load(pe, NX_AT, EXTRA)
            with pe.Fori(0, EXTRA) as b:
                with pe.If(b < n_extra):
                    plan(b + (E + 1))
                    pe.wait_ge(y_ready, b + E)
                    turn_in(b + (E + 1))
                    pe.wait_ge(xT_ready, b + (E + 2))
                    for j in range(KD):
                        up(b + E, j, P)
                    down(b + E)(P)
                with pe.Else():
                    pe.nop()


_INS = ['x', 'norm1_g', 'w_in', 'q_norm_g', 'k_norm_g', 'rel_bias', 'sg_ln_g', 'sg_ln_b', 'sg_w', 'sg_b',
        'w_branch_a', 'w_branch_b', 'w_out', 'norm2_g', 'router_w', 'router_b',
        'w_gate_up', 'b_gate_up', 'w_down', 'b_down']


def kernel(**inputs):
    import numpy as _np
    import concourse.bacc as _bacc
    from concourse import mybir as _mybir
    from concourse.bass_utils import run_bass_kernel_spmd as _run

    nc = _bacc.Bacc("TRN2", target_bir_lowering=False, num_devices=1)
    arrays, args = {}, []
    for name in _INS:
        a = _np.ascontiguousarray(inputs[name])
        arrays[f"in_{name}_dram"] = a
        args.append(nc.dram_tensor(f"in_{name}_dram", a.shape, _mybir.dt.from_np(a.dtype), kind="ExternalInput").ap())
    shape = inputs['x'].shape
    args.append(nc.dram_tensor("out_0_dram", shape, _mybir.dt.from_np(_np.dtype('float32')), kind="ExternalOutput").ap())
    block_kernel(nc, *args)
    r = _run(nc, [arrays], core_ids=[0])
    return r.results[0]["out_0_dram"]
```

```python
from contextlib import ExitStack

import concourse.bass as bass
from concourse import mybir

ALU = mybir.AluOpType
ACT = mybir.ActivationFunctionType
AX_X = mybir.AxisListType.X
F32 = mybir.dt.float32
F32R = mybir.dt.float32r
I32 = mybir.dt.int32
BF16 = mybir.dt.bfloat16
U32 = mybir.dt.uint32

P = 128
SLOTS = 12
RAW = 6
CHUNK = 2048
QUEUE = 3
REG = 2048
NEG = -1e30


def block_kernel(nc, x, norm1_g, w_in, q_norm_g, k_norm_g, rel_bias, sg_ln_g, sg_ln_b, sg_w, sg_b,
                 w_branch_a, w_branch_b, w_out, norm2_g, router_w, router_b,
                 w_gate_up, b_gate_up, w_down, b_down, out):
    _, S, D = x.shape
    H, REL = rel_bias.shape[1:]
    DH = q_norm_g.shape[1]
    G = sg_w.shape[1]
    SGW = sg_ln_g.shape[1]
    AW = H * DH
    E = router_w.shape[2]
    FF = w_down.shape[2]
    TOPK = 4
    CLIP = (REL - 1) // 2
    LIMIT, ALPHA, EPS = 7.0, 1.702, 1e-6
    T = S // P
    KD = D // P
    FT = FF // P
    HP = H // 2
    SIZES = {64: [(64, 0)], 96: [(64, 0), (32, 512)], 128: [(128, 0)]}
    ROUNDS = {64: [(0, 0, 256), (0, 256, 256)], 96: [(0, 0, 512), (1, 0, 256)], 128: [(0, 0, 512), (0, 512, 512)]}
    EXTRA = S * TOPK // P - 1
    PAIRC = 256
    assert T == 4 and KD == 8 and FT == 8 and AW == 512 and SGW == 512 and DH == 64 and G == 4

    UNITS = 8 + 4 + 8 + 8 + 4
    U_BASE, B_BASE, A_BASE, O_BASE = 8, 12, 20, 28
    q0, u0 = 0, 3 * AW
    v0 = u0 + SGW
    ga0, gb0 = u0 + 2 * SGW, u0 + 2 * SGW + D
    chunks = []
    for c in range(2):
        chunks.append(("in", v0 + c * PAIRC, c + 1))
    for c in range(6):
        chunks.append(("in", q0 + c * PAIRC, c + 3))
    for c in range(2):
        chunks.append(("in", u0 + c * PAIRC, U_BASE + 2 * c + 2))
    for kind, base, col in (("b", B_BASE, gb0), ("a", A_BASE, ga0)):
        for half in range(2):
            chunks.append((kind, half * 512, base + 4 * half + 4))
            for c in range(2):
                chunks.append(("in", col + (2 * half + c) * PAIRC, base + 4 * half + 2 * c + 2))
    for c in range(4):
        chunks.append(("o", c * PAIRC, O_BASE + c + 1))
    DENSE = len(chunks)
    SPLIT = ("in", "o")
    N_SPLIT = sum(kind in SPLIT for kind, _, _ in chunks)
    BEFORE_A = 10 + (A_BASE - 1 - U_BASE) // 2
    def slot(c):
        return c % RAW

    def split_number(c):
        return sum(kind in SPLIT for kind, _, _ in chunks[:c])

    def nth_split(n):
        return [c for c, (kind, _, _) in enumerate(chunks) if kind in SPLIT][n]

    UNIT_CHUNK = {}
    for u in range(8):
        UNIT_CHUNK[u] = nth_split(u)
    for u in range(U_BASE, O_BASE):
        UNIT_CHUNK[u] = nth_split(8 + (u - U_BASE) // 2)
    for u in range(O_BASE, UNITS):
        UNIT_CHUNK[u] = DENSE - 4 + u - O_BASE
    BRANCH_CHUNK = {(kind, half): [c for c, (k, _, _) in enumerate(chunks) if k == kind][half]
                    for kind in "ab" for half in range(2)}

    h2_rows = nc.dram_tensor("h2_rows", (S, D), F32, kind="Internal").ap()
    rel_rows = nc.dram_tensor("rel_rows", (H, 5 * P), F32, kind="Internal").ap()

    gu_rows = w_gate_up.rearrange("l e k n -> (l e k) n")
    down_rows = w_down.rearrange("l e k n -> (l e k) n")
    out_rows = out.rearrange("b s d -> (b s) d")
    x_rows = x.rearrange("b s d -> (b s) d")

    with ExitStack() as ctx:
        def sb(name, shape, dt=F32):
            return ctx.enter_context(nc.sbuf_tensor(name, shape, dt))

        def sem(name):
            return ctx.enter_context(nc.semaphore(name))

        with ExitStack() as dense:
            m_lo = dense.enter_context(nc.sbuf_tensor("m_lo", [P, KD, S], F32R))
            m_hi = dense.enter_context(nc.sbuf_tensor("m_hi", [P, KD, S], F32R))
        REGIONS = (9, 10, 6, 7, 0, 1, 4, 5, 8, 11, 12)
        work = sb("work", [P, len(REGIONS) * REG])

        def region(r, off, n):
            at = REGIONS.index(r) * REG + off
            return work[:, at:at + n]

        xin = region(0, 0, 2 * REG).rearrange("p (t d) -> p t d", t=T)
        qk_rows = [region(r, 0, REG).rearrange("p (t n) -> p t n", t=T) for r in (0, 1)]
        merged = region(0, 0, 2 * REG).rearrange("p (m s) -> p m s", m=KD)
        h_full = region(4, 0, 2 * REG).rearrange("p (t k n) -> p t k n", t=T, k=KD)
        qT = region(4, 0, REG).rearrange("p (h s) -> p h s", h=HP)
        kT = region(5, 0, REG).rearrange("p (h s) -> p h s", h=HP)
        vv = region(6, 0, REG).rearrange("p (t n) -> p t n", t=T)
        vn = region(7, 0, REG).rearrange("p (t n) -> p t n", t=T)
        uT = region(8, 0, REG).rearrange("p (g s) -> p g s", g=G)
        relM = region(9, 0, 1024).rearrange("p (b n) -> p b n", b=2)
        srow = region(9, 1024, 1024).rearrange("p (b n) -> p b n", b=2)
        prow = region(10, 0, 1024).rearrange("p (b n) -> p b n", b=2)
        pcol = region(10, 1024, 1024).rearrange("p (b n) -> p b n", b=2)
        scratch = region(11, 0, 1024)
        bias_rows = region(11, 1024, 512).rearrange("p (c n) -> p c n", c=4)
        gate = region(11, 0, 1024).rearrange("p (b n) -> p b n", b=2)
        gated = region(11, 1024, 512)
        ln_g = region(12, 0, 512)
        ln_b = region(12, 512, 512)
        sgb = region(12, 1024, 512).rearrange("p (g n) -> p g n", g=G)
        wT = region(12, 1536, 512).rearrange("p (g n) -> p g n", g=G)
        sgw_rows = region(10, 0, 512).rearrange("p (g n) -> p g n", g=G)
        rel_in = region(9, 1024, REL)
        rel_out = region(10, 1024, 5 * P)
        rw = region(12, 1024, KD * E).rearrange("p (k e) -> p k e", k=KD)
        h2 = region(6, 0, 2 * REG).rearrange("p (t d) -> p t d", t=T)
        h2T = region(4, 0, 2 * REG).rearrange("p (k s) -> p k s", k=KD)
        rt = region(0, 0, 2 * REG)
        TE = T * E
        logits, weight, hit, before, place_a = (
            rt[:, n * TE:(n + 1) * TE].rearrange("p (t e) -> p t e", t=T) for n in range(5))
        hits = rt[:, 1280:1280 + TOPK * TE].rearrange("p (t k e) -> p t k e", t=T, k=TOPK)
        rb_all = region(8, 768, E)
        iota_e = region(8, 768 + E, E)
        top = rt[:, 1024:1024 + 8 * T].rearrange("p (t k) -> p t k", t=T)
        top_i = rt[:, 1056:1056 + 8 * T].rearrange("p (t k) -> p t k", t=T).bitcast(U32)
        top_f = rt[:, 1088:1088 + 8 * T].rearrange("p (t k) -> p t k", t=T)
        prob = rt[:, 1120:1120 + TOPK * T].rearrange("p (t k) -> p t k", t=T)
        psum_t = rt[:, 1140:1140 + T]
        neg_t = rt[:, 1144:1144 + T]
        col_cnt = rt[0:E, 1150:1151]
        col_fl = rt[0:E, 1152:1155]
        col_nb = rt[0:E, 1156:1157]
        col_base = rt[0:E, 1158:1159]
        col_eb = rt[0:E, 1160:1162]
        col_code = rt[0:E, 1164:1165]
        oh_x = rt[0:E, 1170:1170 + 3 * (EXTRA + 1)].rearrange("p (b j) -> p b j", b=3)
        xg = region(9, 0, 1024)
        yrow = region(9, 1024, 1024)
        xt = region(10, 0, 1024)
        hh = region(10, 1024, 1024)
        gs = region(11, 0, 1024)
        us = region(11, 1024, 1024)
        eg = region(7, 0, 1024)
        eu = region(7, 1024, 1024)
        es = region(6, 0, 1024)
        slots_128 = region(8, 0, 512)
        slots_64 = region(8, 512, P)
        slots_32 = region(8, 640, P)
        more_64 = region(8, 1536, P)
        more_32 = region(8, 1664, P)
        onehot = region(8, 1024, 512).bitcast(BF16).rearrange("p (b t n) -> p b t n", b=2, t=T)
        wTe = region(6, 1024, 512)
        bd_rows = region(1, 0, 1024)

        ident = sb("ident", [P, P])
        ones = sb("ones", [P, P])
        before_m = sb("before_m", [P, P])
        rows = sb("rows", [P, P])
        colT = sb("colT", [P, 10 + KD])
        bguT = sb("bguT", [P, E * 2 * FT])
        eps = sb("eps", [P, 1])
        stat = sb("stat", [P, 16])
        rstd = sb("rstd", [P, 16])
        mean = sb("mean", [P, 8])
        smax = sb("smax", [P, 2])
        nmax = sb("nmax", [P, 2])
        ssum = sb("ssum", [P, 2])
        rsum = sb("rsum", [P, 2])
        pos = sb("pos", [P, T, E])
        VALS = 5
        vals = sb("vals", [P, T, E, VALS], BF16)
        val_e = sb("val_e", [P, T, VALS], BF16)
        chosen = sb("chosen", [P, T, E], BF16)
        ones_b = sb("ones_b", [P, P], BF16)
        before_b = sb("before_b", [P, P], BF16)
        tok_f = sb("tok_f", [P, 2])
        tile_0 = sb("tile_0", [P, T])
        copy_no = sb("copy_no", [P, 2])
        plan_i = sb("plan_i", [P, 6], I32)
        plan_w = sb("plan_w", [P, 6])
        tokn = sb("tokn", [P, T])
        table = sb("table", [1, 80], I32)
        N_AT, XE_AT, XB_AT, NX_AT = 0, E, E + EXTRA + 1, E + 2 * (EXTRA + 1)

        with ExitStack() as dense:
            raw = dense.enter_context(nc.sbuf_tensor("raw", [P, RAW, CHUNK], F32))
            w_hi = dense.enter_context(nc.sbuf_tensor("w_hi", [P, 2, CHUNK], F32R))
            w_lo = dense.enter_context(nc.sbuf_tensor("w_lo", [P, 2, CHUNK], F32R))
            hT_lo = dense.enter_context(nc.sbuf_tensor("hT_lo", [P, KD, S], F32R))
            hT_hi = dense.enter_context(nc.sbuf_tensor("hT_hi", [P, KD, S], F32R))
        ring = sb("ring", [P, SLOTS, CHUNK])
        x2 = sb("x2", [P, T, D])

        PJ = ctx.enter_context(nc.psum_tensor("PJ", [P, 2, 1024], F32))
        SBK = ctx.enter_context(nc.psum_tensor("SBK", [P, 2, 512], F32))
        TT = ctx.enter_context(nc.psum_tensor("TT", [P, 1024], F32))
        PT, PV = TT[:, 0:512], TT[:, 512:1024]
        YD = SBK[:, :, :].rearrange("p b n -> p (b n)")

        arrived = [sem(f"arrived{j}") for j in range(SLOTS)]
        raw_in = [sem(f"raw_in{j}") for j in range(RAW)]
        w_hi_ready, w_split = sem("w_hi_ready"), sem("w_split")
        h_full_ready, h_hi_ready = sem("h_full_ready"), sem("h_hi_ready")
        m_hi_ready, m_split = sem("m_hi_ready"), sem("m_split")
        x_in = [sem(f"x_in{t}") for t in range(T)]
        rows_in, gains_in, bias_in, sgw_in, rel_in_s, ln_in = (sem(n) for n in
            ("rows_in", "gains_in", "bias_in", "sgw_in", "rel_in_s", "ln_in"))
        rel_stored, relM_in, x_again, late_in = (sem(n) for n in ("rel_stored", "relM_in", "x_again", "late_in"))
        pool_made = sem("pool_made")
        sgw_masked = sem("sgw_masked")
        relM_ready = sem("relM_ready")
        cols_turned, cols_ready = sem("cols_turned"), sem("cols_ready")
        gains_turned, gains_ready = sem("gains_turned"), sem("gains_ready")
        bias_turned, bias_ready = sem("bias_turned"), sem("bias_ready")
        sgw_turned, wT_ready = sem("sgw_turned"), sem("wT_ready")
        x_sq, x_std, xs_ready, x_turned, hT_ready = (sem(n) for n in
            ("x_sq", "x_std", "xs_ready", "x_turned", "hT_ready"))
        rel_ready = sem("rel_ready")
        unit_ready = sem("unit_ready")
        unit_free = [sem(f"unit_free{b}") for b in range(2)]
        qk_sq, qk_var, qk_std = sem("qk_sq"), sem("qk_var"), sem("qk_std")
        qk_turned, qk_ready = sem("qk_turned"), sem("qk_ready")
        vc_ready, vc_sq, v_var, v_std, vn_ready = (sem(n) for n in
            ("vc_ready", "vc_sq", "v_var", "v_std", "vn_ready"))
        mixed, sgu_ready = sem("mixed"), sem("sgu_ready")
        scores_ready, smax_ready, exp_ready, probs_ready = (sem(n) for n in
            ("scores_ready", "smax_ready", "exp_ready", "probs_ready"))
        probs_turned, pcol_ready, pv_done, attn_ready = (sem(n) for n in
            ("probs_turned", "pcol_ready", "pv_done", "attn_ready"))
        gate_ready, merged_ready = sem("gate_ready"), sem("merged_ready")
        x2_ready, x2_sq, x2_var, x2_std, x2_rstd, h2_ready = (sem(n) for n in
            ("x2_ready", "x2_sq", "x2_var", "x2_std", "x2_rstd", "h2_ready"))
        h2_stored, out_stored = sem("h2_stored"), sem("out_stored")
        h2_turned, h2T_ready, logits_ready = sem("h2_turned"), sem("h2T_ready"), sem("logits_ready")
        top_ready, top_exp, chosen_ready, counted = (sem(n) for n in
            ("top_ready", "top_exp", "chosen_ready", "counted"))
        extra_cols, extra_base, extra_hot, extra_ready, routed, counts_there = (sem(n) for n in
            ("extra_cols", "extra_base", "extra_hot", "extra_ready", "routed", "counts_there"))
        hot_ready, plan_there, plan_ready = sem("hot_ready"), sem("plan_there"), sem("plan_ready")
        gathered, xg_turned, xT_ready = sem("gathered"), sem("xg_turned"), sem("xT_ready")
        gu_ready, chunk_used, gs_ready, us_ready, turned, turned_read, g_ready, s_ready, hh_ready = (sem(n) for n in
            ("gu_ready", "chunk_used", "gs_ready", "us_ready", "turned", "turned_read", "g_ready", "s_ready", "hh_ready"))
        yd_ready, y_ready, scattered = (sem(n) for n in ("yd_ready", "y_ready", "scattered"))
        plan_taken, first_used = sem("plan_taken"), sem("first_used")
        weights_turned, wTe_ready, bd_in, bias_added, biased = (sem(n) for n in
            ("weights_turned", "wTe_ready", "bd_in", "bias_added", "biased"))
        dve_chain, act_chain, waits_met = sem("dve_chain"), sem("act_chain"), sem("waits_met")

        def free_before(u):
            return u // 2

        def by_rows(eng, count, body):
            with eng.If(count < 65):
                body(64)
            with eng.Else():
                with eng.If(count < 97):
                    body(96)
                with eng.Else():
                    body(128)
                eng.nop()

        def turned_at(size, n_):
            return (512 * n_, 512 * n_ + 256) if size == 64 else (0, 512)

        def folded(rows_, b):
            return rows_.rearrange("s (j n) -> (s j) n", j=P // b)

        def settle(eng):
            eng.sem_inc(waits_met, 1)

        def load(eng, at, most):
            return eng.value_load(table[0:1, bass.ds(at, 1)], min_val=0, max_val=most)

        def rows_left(eng, b):
            return load(eng, load(eng, b + XE_AT, E - 1) + N_AT, S) - load(eng, b + XB_AT, 3) * P

        block = ctx.enter_context(nc.Block())

        @block.sync
        def _(sp):
            for t in range(T):
                sp.dma_start(xin[:, t, :], x_rows[t * P:(t + 1) * P, :]).then_inc(x_in[t], 16)

            def through(c):
                if chunks[c][0] in SPLIT:
                    sp.wait_ge(w_split, split_number(c) + 1)
                else:
                    sp.wait_ge(unit_ready, chunks[c][2])

            for c, (kind, col, _) in enumerate(chunks):
                if c >= RAW:
                    through(c - RAW)
                if kind == "in":
                    src, n = w_in[0, :, col:col + PAIRC], PAIRC
                elif kind == "o":
                    src, n = w_out[0, :, col:col + PAIRC], PAIRC
                else:
                    src, n = (w_branch_a if kind == "a" else w_branch_b)[0, :, col:col + 512], 512
                sp.dma_start(raw[:, slot(c), :].rearrange("p (k n) -> p k n", n=n),
                             src.rearrange("(k p) n -> p k n", p=P)).then_inc(raw_in[slot(c)], 16)

            def used(i, j):
                if j in (0, KD - 1, SLOTS - 1):
                    sp.wait_ge({0: first_used, KD - 1: gu_ready, SLOTS - 1: yd_ready}[j], i + 1)
                else:
                    sp.wait_ge(chunk_used, i * (SLOTS - 3) + (j if j < KD else j - 1))

            def short_queue(i, j):
                if j >= QUEUE:
                    sp.wait_ge(arrived[j - QUEUE], i * 16 + 16)
                else:
                    at = SLOTS + j - QUEUE
                    sp.wait_ge(arrived[at], i * 16)

            def expert_chunk(e, j):
                if j < KD:
                    sp.dma_start(ring[:, j, :], gu_rows[bass.ds(e * D + j * P, P), :]).then_inc(arrived[j], 16)
                else:
                    sp.dma_start(ring[:, j, :].rearrange("p (c n) -> p c n", c=2),
                                 down_rows[bass.ds(e * FF + (j - KD) * 2 * P, 2 * P), :]
                                 .rearrange("(c p) n -> p c n", p=P)).then_inc(arrived[j], 16)

            sp.wait_ge(unit_ready, O_BASE)
            sp.wait_ge(x_again, 16 * T)
            for j in range(RAW + 4, SLOTS):
                expert_chunk(0, j)
            for c in range(DENSE - RAW, DENSE):
                through(c)
                expert_chunk(0, slot(c))
            sp.wait_ge(unit_ready, UNITS)
            for j in range(RAW, RAW + 4):
                expert_chunk(0, j)
            for t in range(T):
                sp.wait_ge(h2_ready, t + 1)
                sp.dma_start(h2_rows[t * P:(t + 1) * P, :], h2[:, t, :]).then_inc(h2_stored, 16)
            with sp.Fori(1, E) as i:
                for j in range(SLOTS):
                    used(i - 1, j)
                    settle(sp)
                    short_queue(i, j)
                    expert_chunk(i, j)
            sp.wait_ge(routed, 1)
            n_extra = load(sp, NX_AT, EXTRA)
            with sp.Fori(0, EXTRA) as b:
                with sp.If(b < n_extra):
                    e = load(sp, b + XE_AT, E - 1)
                    for j in range(SLOTS):
                        used(b + (E - 1), j)
                        settle(sp)
                        short_queue(b + E, j)
                        expert_chunk(e, j)
                with sp.Else():
                    sp.nop()

        @block.gpsimd
        def _(pool):
            made = [0]

            def link(ins):
                made[0] += 1
                ins.then_inc(pool_made, 1)
                pool.wait_ge(pool_made, made[0])

            link(nc.gpsimd.memset(ident[:], 0.0))
            link(nc.gpsimd.memset(ones[:], 1.0))
            link(nc.gpsimd.affine_select(out=ident[:], in_=ident[:], compare_op=ALU.not_equal, fill=1.0,
                                         base=0, pattern=[[-1, P]], channel_multiplier=1))
            link(nc.gpsimd.affine_select(out=before_m[:], in_=ones[:], compare_op=ALU.is_gt, fill=0.0,
                                         base=0, pattern=[[1, P]], channel_multiplier=-1))
            link(nc.gpsimd.iota(tokn[:], pattern=[[P, T]], base=0, channel_multiplier=1,
                                allow_small_or_imprecise_dtypes=True))
            link(nc.gpsimd.iota(tile_0[:], pattern=[[P, T]], base=0, channel_multiplier=0,
                                allow_small_or_imprecise_dtypes=True))
            pool.dma_start(ln_g, sg_ln_g[0:1, :].to_broadcast([P, SGW])).then_inc(ln_in, 16)
            pool.dma_start(ln_b, sg_ln_b[0:1, :].to_broadcast([P, SGW])).then_inc(ln_in, 16)
            pool.dma_start(sgb.rearrange("p g n -> p (g n)"),
                           sg_b.rearrange("l g n -> l (g n)").to_broadcast([P, SGW])).then_inc(ln_in, 16)
            pool.wait_ge(w_hi_ready, 1)
            nc.gpsimd.tensor_tensor(w_lo[:, 0, :], raw[:, 0, :], w_hi[:, 0, :].bitcast(F32),
                                    ALU.subtract).then_inc(w_split, 1)
            pool.wait_ge(sgw_in, 16)
            nc.gpsimd.affine_select(out=sgw_rows, in_=sgw_rows, compare_op=ALU.is_ge, fill=0.0, base=0,
                                    pattern=[[0, G], [-1, P]], channel_multiplier=1).then_inc(sgw_masked, 1)
            pool.wait_ge(rel_stored, 16)
            pool.wait_ge(wT_ready, 1)
            for h in range(H):
                if h >= 2:
                    pool.wait_ge(smax_ready, T * (h - 1))
                src = bass.AP(rel_rows.tensor, h * 5 * P, [[1, P], [1, 4 * P]])
                pool.dma_start(relM[:, h % 2, :], src).then_inc(relM_in, 16)
                pool.wait_ge(relM_in, 16 * (h + 1))
                nc.gpsimd.memset(relM[0:64, h % 2, 0:64], NEG).then_inc(relM_ready, 1)
            pool.wait_ge(unit_ready, A_BASE)
            for table_, base, pattern in ((slots_128, 0, [[1, S]]), (slots_64, 0, [[0, 2], [1, 64]]),
                                          (slots_32, 64, [[0, 4], [1, 32]])):
                link(nc.gpsimd.iota(table_, pattern=pattern, base=base, channel_multiplier=0,
                                    allow_small_or_imprecise_dtypes=True))
            link(nc.gpsimd.memset(region(8, 1024, 1024), 0.0))
            for j in range(4):
                link(nc.gpsimd.memset(copy_no[32 * j:32 * j + 32, 0:1], float(j // 2)))
                link(nc.gpsimd.memset(copy_no[32 * j:32 * j + 32, 1:2], float(j)))
            link(nc.gpsimd.iota(iota_e, pattern=[[1, E]], base=0, channel_multiplier=0,
                                allow_small_or_imprecise_dtypes=True))
            pool.dma_start(rb_all, router_b[0:1, :].to_broadcast([P, E])).then_inc(late_in, 16)
            pool.dma_start(rw, router_w[0].rearrange("(k p) e -> p k e", p=P)).then_inc(late_in, 16)
            pool.wait_ge(unit_ready, O_BASE)
            for t in range(T):
                pool.dma_start(x2[:, t, :], x_rows[t * P:(t + 1) * P, :]).then_inc(x_again, 16)
            pool.wait_ge(unit_ready, UNITS)
            pool.dma_start(bd_rows[0:E, :], b_down[0]).then_inc(bd_in, 16)
            pool.wait_ge(h2_stored, 16 * T)
            pool.wait_ge(counts_there, 1)

            def gather(n, item, first=False):
                def go(size):
                    blocks = SIZES[size]
                    for n_, (b, off) in enumerate(blocks):
                        nc.gpsimd.indirect_dma_start(
                            out=xg[:, off:off + D * b // P], out_offset=None, in_=folded(h2_rows, b),
                            in_offset=bass.IndirectOffsetOnAxis(ap=plan_i[:, n_:n_ + 1], axis=0)) \
                            .then_inc(gathered, 32 // len(blocks))
                pool.wait_ge(plan_ready, item + 1)
                if not first:
                    pool.wait_ge(xg_turned, item)
                settle(pool)
                by_rows(pool, n, go)

            def scatter(n, item, first=False):
                def go(size):
                    blocks = SIZES[size]
                    for n_, (b, off) in enumerate(blocks):
                        nc.gpsimd.indirect_dma_start(
                            out=folded(out_rows, b),
                            out_offset=bass.IndirectOffsetOnAxis(ap=plan_i[:, 4 + n_:5 + n_], axis=0),
                            in_=yrow[:, off:off + D * b // P], in_offset=None, compute_op=ALU.add) \
                            .then_inc(scattered, 32 // len(blocks))
                pool.wait_ge(y_ready, item + 1)
                if first:
                    pool.wait_ge(out_stored, 16 * T)
                else:
                    pool.wait_ge(scattered, item * 32)
                settle(pool)
                by_rows(pool, n, go)

            gather(load(pool, N_AT, S), 0, first=True)
            gather(load(pool, N_AT + 1, S), 1)
            for t in range(T):
                pool.wait_ge(biased, t + 1)
                pool.dma_start(out_rows[t * P:(t + 1) * P, :], x2[:, t, :]).then_inc(out_stored, 16)
            scatter(load(pool, N_AT, S), 0, first=True)
            with pool.Fori(1, E - 1) as i:
                n, nn = load(pool, i + N_AT, S), load(pool, i + (N_AT + 1), S)
                gather(nn, i + 1)
                scatter(n, i)
            pool.wait_ge(routed, 1)
            gather(rows_left(pool, 0), E)
            scatter(load(pool, N_AT + E - 1, S), E - 1)
            n_extra = load(pool, NX_AT, EXTRA)
            with pool.Fori(0, EXTRA) as b:
                with pool.If(b < n_extra):
                    n, nn = rows_left(pool, b), rows_left(pool, b + 1)
                    gather(nn, b + (E + 1))
                    scatter(n, b + E)
                with pool.Else():
                    pool.nop()
            pool.wait_ge(gathered, n_extra * 32 + (E + 1) * 32)
            pool.wait_ge(scattered, n_extra * 32 + E * 32)

        @block.scalar
        def _(act):
            made = [0]

            def link(ins):
                made[0] += 1
                ins.then_inc(act_chain, 1)
                act.wait_ge(act_chain, made[0])

            act.dma_start(rows[0:KD, :], norm1_g.rearrange("l (k p) -> (l k) p", p=P)).then_inc(rows_in, 16)

            def x_root(t):
                act.wait_ge(x_sq, t + 1)
                nc.scalar.activation(rstd[:, t:t + 1], stat[:, t:t + 1], ACT.Sqrt, bias=eps[:, 0:1],
                                     scale=1.0 / D).then_inc(x_std, 1)

            def h_high(t):
                act.wait_ge(h_full_ready, t + 1)
                nc.scalar.activation(hT_hi[:, :, t * P:(t + 1) * P], h_full[:, t, :, :], ACT.Copy).then_inc(h_hi_ready, 1)

            def w_high(n):
                c = nth_split(n)
                act.wait_ge(raw_in[slot(c)], 16 * (c // RAW + 1))
                if n >= 2:
                    act.wait_ge(unit_ready, chunks[nth_split(n - 2)][2])
                nc.scalar.activation(w_hi[:, n % 2, :], raw[:, slot(c), :], ACT.Copy).then_inc(w_hi_ready, 1)

            x_root(0)
            x_root(1)
            x_root(2)
            h_high(0)
            w_high(0)
            x_root(3)
            h_high(1)
            h_high(2)
            h_high(3)
            w_high(1)
            act.wait_ge(cols_turned, 1)
            for r, g in ((KD, q_norm_g), (KD + 1, k_norm_g)):
                for half in range(2):
                    act.dma_start(rows[r:r + 1, half * DH:(half + 1) * DH], g[0:1, :]).then_inc(gains_in, 16)
            act.dma_start(rows[KD + 2:2 * KD + 2, :], norm2_g.rearrange("l (k p) -> (l k) p", p=P)).then_inc(gains_in, 16)
            act.dma_start(sgw_rows, sg_w[0].rearrange("g t s -> t g s")).then_inc(sgw_in, 16)
            act.dma_start(rel_in[0:H, :], rel_bias[0]).then_inc(rel_in_s, 16)
            act.dma_start(bias_rows[:, 0:4, :], b_gate_up.rearrange("l e (m p) -> (l e m) p", p=P)
                          .rearrange("(c r) p -> r c p", r=P)).then_inc(bias_in, 16)
            for u in range(2):
                w_high(u + 2)
                act.wait_ge(unit_ready, u + 1)
                nc.scalar.activation(vn[:, :, u * PAIRC:(u + 1) * PAIRC],
                                     PJ[:, u % 2, :].rearrange("p (t n) -> p t n", t=T),
                                     ACT.Gelu_apprx_tanh).then_inc(unit_free[u % 2], 1)
                act.wait_ge(vc_ready, u + 1)
                nc.scalar.activation(scratch, vn[:, :, u * PAIRC:(u + 1) * PAIRC], ACT.Square).then_inc(vc_sq, 1)
                act.wait_ge(v_var, u + 1)
                nc.scalar.activation(rstd[:, 8 * u:8 * u + 8], stat[:, 8 * u:8 * u + 8], ACT.Sqrt, bias=eps[:, 0:1],
                                     scale=1.0 / P).then_inc(v_std, 1)
            act.wait_ge(rel_ready, 1)
            act.dma_start(rel_rows[:, :], rel_out[0:H, :]).then_inc(rel_stored, 16)
            for n in range(4):
                u = n + 2
                w_high(u + 2)
                act.wait_ge(unit_ready, u + 1)
                if n:
                    act.wait_ge(qk_var, n)
                else:
                    act.wait_ge(vn_ready, 2)
                nc.scalar.activation(scratch, PJ[:, u % 2, :], ACT.Square).then_inc(qk_sq, 1)
                act.wait_ge(qk_var, n + 1)
                if n:
                    act.wait_ge(unit_free[(u - 1) % 2], (u - 1) // 2 + 1)
                nc.scalar.activation(rstd[:, 0:16], stat[:, 0:16], ACT.Sqrt, bias=eps[:, 0:1],
                                     scale=1.0 / DH).then_inc(qk_std, 1)
                if n == 2:
                    act.wait_ge(bias_turned, 1)
                    nc.scalar.activation(bguT[:], TT[:, 0:512], ACT.Copy).then_inc(bias_ready, 1)
                    act.wait_ge(sgw_turned, 1)
                    nc.scalar.activation(wT, SBK[:, 1, :].rearrange("p (g n) -> p g n", g=G),
                                         ACT.Copy).then_inc(wT_ready, 1)
            for u in (6, 7):
                w_high(u + 2)
                act.wait_ge(unit_ready, u + 1)
                nc.scalar.activation(vv[:, :, (u - 6) * PAIRC:(u - 5) * PAIRC],
                                     PJ[:, u % 2, :].rearrange("p (t n) -> p t n", t=T),
                                     ACT.Copy).then_inc(unit_free[u % 2], 1)
            for u in range(U_BASE, B_BASE):
                if u % 2:
                    w_high(10 + (u - U_BASE) // 2)
                act.wait_ge(unit_ready, u + 1)
                nc.scalar.activation(uT[:, u - U_BASE, :], PJ[:, u % 2, 0:512],
                                     ACT.Gelu_apprx_tanh).then_inc(unit_free[u % 2], 1)

            def attend(s):
                if s < T * H:
                    a, n = s, (s % T + 1) * P
                    act.wait_ge(smax_ready, a + 1)
                    if a >= 2:
                        act.wait_ge(probs_turned, a - 1)
                    nc.scalar.activation(prow[:, a % 2, 0:n], srow[:, a % 2, 0:n], ACT.Exp,
                                         bias=nmax[:, a % 2:a % 2 + 1],
                                         accum_out=ssum[:, a % 2:a % 2 + 1]).then_inc(exp_ready, 1)
                if 2 <= s < T * H + 2:
                    a, n = s - 2, ((s - 2) % T + 1) * P
                    act.wait_ge(probs_turned, a + 1)
                    if a >= 2:
                        act.wait_ge(pv_done, a - 1)
                    nc.scalar.activation(pcol[:, a % 2, 0:n], PT[:, 0:n], ACT.Copy).then_inc(pcol_ready, 1)
                if s >= 3 and (s - 3) % 8 == 7:
                    hp = (s - 3) // 8
                    act.wait_ge(pv_done, 8 * (hp + 1))
                    nc.scalar.activation(qT[:, hp, :], PV, ACT.Copy).then_inc(attn_ready, 1)

            def open_gate(u):
                n = u - B_BASE
                if A_BASE < u < O_BASE - 1 and u % 2:
                    w_high(10 + (u - U_BASE) // 2)
                act.wait_ge(unit_ready, u + 1)
                if n >= 2:
                    act.wait_ge(merged_ready, n - 1)
                nc.scalar.activation(gate[:, n % 2, :], PJ[:, u % 2, 0:512], ACT.Sigmoid).then_inc(gate_ready, 1)

            act.wait_ge(vn_ready, 2)
            for s in range(T * H + 3):
                attend(s)
                if 8 < s < T * H and s % 8 == 1:
                    w_high(11 + s // 8)
                if s < T * H and s % 4 == 3:
                    open_gate(B_BASE + s // 4)
            for m in range(KD):
                open_gate(A_BASE + m)
                if m == 0:
                    w_high(BEFORE_A)
                act.wait_ge(merged_ready, KD + m + 1)
                nc.scalar.activation(m_hi[:, m, :], merged[:, m, :], ACT.Copy).then_inc(m_hi_ready, 1)
            w_high(N_SPLIT - 3)
            link(nc.scalar.activation(ssum[:, 0:1], eps[:, 0:1], ACT.Sqrt))
            w_high(N_SPLIT - 2)
            w_high(N_SPLIT - 1)
            for k in range(KD):
                act.wait_ge(h2_turned, k + 1)
                nc.scalar.activation(h2T[:, k, :], SBK[:, k % 2, :], ACT.Copy,
                                     scale=colT[:, KD + 2 + k:KD + 3 + k]).then_inc(h2T_ready, 1)
            act.wait_ge(x2_var, 1)
            nc.scalar.activation(rstd[:, 0:T], mean[:, 0:T], ACT.Sqrt, bias=eps[:, 0:1],
                                 scale=1.0 / D).then_inc(x2_std, 1)
            act.wait_ge(x2_rstd, 1)
            for t in range(T - 1):
                nc.scalar.activation(h2[:, t, :], x2[:, t, :], ACT.Copy, scale=rstd[:, t:t + 1]).then_inc(h2_ready, 1)
            for t in range(T):
                act.wait_ge(top_ready, 1)
                nc.scalar.activation(prob[:, t, :], top[:, t, 0:TOPK], ACT.Exp, bias=neg_t[:, t:t + 1],
                                     accum_out=psum_t[:, t:t + 1]).then_inc(top_exp, 1)
            nc.scalar.activation(h2[:, T - 1, :], x2[:, T - 1, :], ACT.Copy, scale=rstd[:, T - 1:T]).then_inc(h2_ready, 1)
            act.wait_ge(counts_there, 1)

            def gate_rows(item):
                def go(size):
                    for n_, (blk, c0, w) in enumerate(ROUNDS[size]):
                        o = SIZES[size][blk][1] + c0
                        if n_ == 0:
                            act.wait_ge(gu_ready, item + 1)
                        nc.scalar.activation(gs[:, o:o + w], PJ[:, 0, o:o + w], ACT.Copy).then_inc(gs_ready, 1)
                return go

            def sigmoids(item):
                def go(size):
                    for n_, (blk, c0, w) in enumerate(ROUNDS[size]):
                        o = SIZES[size][blk][1] + c0
                        act.wait_ge(g_ready, item * 2 + (n_ + 1))
                        nc.scalar.activation(es[:, o:o + w], eg[:, o:o + w], ACT.Sigmoid, scale=ALPHA).then_inc(s_ready, 1)
                return go

            def results(item):
                def go(size):
                    act.wait_ge(yd_ready, item + 1)
                    act.wait_ge(plan_taken, item + 1)
                    for n_, (b, off) in enumerate(SIZES[size]):
                        w = D * b // P
                        last = nc.scalar.activation(yrow[:, off:off + w], YD[:, off:off + w], ACT.Copy,
                                                    scale=plan_w[:, 4 + n_:5 + n_])
                    last.then_inc(y_ready, 1)
                return go

            act.wait_ge(weights_turned, 1)
            act.wait_ge(h2_stored, 16 * T)
            nc.scalar.activation(wTe[0:E, :], TT[0:E, 0:512], ACT.Copy).then_inc(wTe_ready, 1)

            def item(i, n):
                by_rows(act, n, lambda size: (gate_rows(i)(size), sigmoids(i)(size), results(i)(size)))

            item(0, load(act, N_AT, S))
            with act.Fori(1, E) as i:
                item(i, load(act, i + N_AT, S))
            act.wait_ge(routed, 1)
            n_extra = load(act, NX_AT, EXTRA)
            with act.Fori(0, EXTRA) as b:
                with act.If(b < n_extra):
                    item(b + E, rows_left(act, b))
                with act.Else():
                    act.nop()

        @block.vector
        def _(dve):
            made = [0]

            def link(ins):
                made[0] += 1
                ins.then_inc(dve_chain, 1)
                dve.wait_ge(dve_chain, made[0])

            def t_major(ap):
                return ap.rearrange("p (t n) -> p t n", t=T)

            link(nc.vector.memset(eps[:], EPS))
            link(nc.vector.memset(plan_i[:], 0))
            def x_normed(t):
                dve.wait_ge(x_in[t], 16)
                if t:
                    dve.wait_ge(x_sq, t)
                nc.vector.tensor_tensor_reduce(scratch, xin[:, t, :], xin[:, t, :], 1.0, 0.0, ALU.mult, ALU.add,
                                               stat[:, t:t + 1]).then_inc(x_sq, 1)
                dve.wait_ge(x_std, t + 1)
                link(nc.vector.reciprocal(rstd[:, t:t + 1], rstd[:, t:t + 1]))
                nc.vector.tensor_scalar(xin[:, t, :], xin[:, t, :], rstd[:, t:t + 1], None,
                                        ALU.mult).then_inc(xs_ready, 1)

            def h_gained(t):
                dve.wait_ge(x_turned, t + 1)
                nc.vector.tensor_tensor(h_full[:, t, :, :],
                                        (PJ[:, 1, :] if t % 2 else TT[:, :]).rearrange("p (k n) -> p k n", k=KD),
                                        colT[:, 0:KD].unsqueeze(2).to_broadcast([P, KD, P]),
                                        ALU.mult).then_inc(h_full_ready, 1)

            def h_low(t):
                dve.wait_ge(h_full_ready, t + 1)
                dve.wait_ge(h_hi_ready, t + 1)
                nc.vector.tensor_tensor(hT_lo[:, :, t * P:(t + 1) * P], h_full[:, t, :, :],
                                        hT_hi[:, :, t * P:(t + 1) * P].bitcast(F32), ALU.subtract).then_inc(hT_ready, 1)

            def w_low(n):
                c = nth_split(n)
                dve.wait_ge(w_hi_ready, n + 1)
                nc.vector.tensor_tensor(w_lo[:, n % 2, :], raw[:, slot(c), :], w_hi[:, n % 2, :].bitcast(F32),
                                        ALU.subtract).then_inc(w_split, 1)

            x_normed(0)
            x_normed(1)
            dve.wait_ge(cols_turned, 1)
            link(nc.vector.tensor_copy(colT[:, 0:KD], SBK[:, 0, 0:KD]))
            nc.vector.engine_nop().then_inc(cols_ready, 1)
            h_gained(0)
            x_normed(2)
            h_gained(1)
            h_low(0)
            x_normed(3)
            h_gained(2)
            h_low(1)
            h_gained(3)
            h_low(2)
            h_low(3)
            dve.wait_ge(w_split, 1)
            w_low(1)

            def turned_qk(n):
                dve.wait_ge(qk_turned, n + 1)
                is_k, hp = divmod(n, HP)
                nc.vector.tensor_scalar((kT if is_k else qT)[:, hp, :], SBK[:, n % 2, :],
                                        colT[:, KD + is_k:KD + is_k + 1],
                                        1.0 if is_k else float(DH) ** -0.5, ALU.mult, ALU.mult).then_inc(qk_ready, 1)

            dve.wait_ge(ln_in, 48)
            for c in range(2):
                w_low(c + 2)
                dve.wait_ge(unit_free[c], 1)
                part = vn[:, :, c * PAIRC:(c + 1) * PAIRC].rearrange("p t (g n) -> p t g n", n=P)
                bc = [P, T, 2, P]
                if c:
                    dve.wait_ge(v_std, c)
                link(nc.vector.tensor_reduce(mean[:, 0:8].rearrange("p (t g) -> p t g", t=T), part, AX_X, ALU.add))
                link(nc.vector.tensor_scalar(mean[:, 0:8], mean[:, 0:8], 1.0 / P, None, ALU.mult))
                nc.vector.tensor_tensor(part, part, mean[:, 0:8].rearrange("p (t g) -> p t g", t=T).unsqueeze(3)
                                        .to_broadcast(bc), ALU.subtract).then_inc(vc_ready, 1)
                dve.wait_ge(vc_sq, c + 1)
                nc.vector.tensor_reduce(stat[:, 8 * c:8 * c + 8], scratch.rearrange("p (a n) -> p a n", n=P),
                                        AX_X, ALU.add).then_inc(v_var, 1)
                dve.wait_ge(v_std, c + 1)
                link(nc.vector.reciprocal(rstd[:, 8 * c:8 * c + 8], rstd[:, 8 * c:8 * c + 8]))
                link(nc.vector.tensor_tensor(part, part, rstd[:, 8 * c:8 * c + 8].rearrange("p (t g) -> p t g", t=T)
                                             .unsqueeze(3).to_broadcast(bc), ALU.mult))
                cols = slice(c * PAIRC, (c + 1) * PAIRC)
                link(nc.vector.tensor_tensor(vn[:, :, cols], vn[:, :, cols],
                                             ln_g[:, cols].unsqueeze(1).to_broadcast([P, T, PAIRC]), ALU.mult))
                nc.vector.tensor_tensor(vn[:, :, cols], vn[:, :, cols],
                                        ln_b[:, cols].unsqueeze(1).to_broadcast([P, T, PAIRC]),
                                        ALU.add).then_inc(vn_ready, 1)
            dve.wait_ge(rel_in_s, 16)
            own = CLIP + P
            link(nc.vector.tensor_copy(rel_out[0:H, 0:own], rel_in[0:H, REL - own:REL]))
            nc.vector.tensor_copy(rel_out[0:H, own:5 * P],
                                  rel_in[0:H, REL - 1:REL].to_broadcast([H, 5 * P - own])).then_inc(rel_ready, 1)
            for n in range(4):
                u = n + 2
                w_low(u + 2)
                dve.wait_ge(qk_sq, n + 1)
                if n:
                    dve.wait_ge(qk_std, n)
                nc.vector.tensor_reduce(stat[:, 0:16], scratch.rearrange("p (a n) -> p a n", n=DH),
                                        AX_X, ALU.add).then_inc(qk_var, 1)
                dve.wait_ge(qk_std, n + 1)
                link(nc.vector.reciprocal(rstd[:, 0:16], rstd[:, 0:16]))
                dst = qk_rows[n // 2][:, :, (n % 2) * PAIRC:(n % 2 + 1) * PAIRC]
                nc.vector.tensor_tensor(dst.rearrange("p t (h n) -> p t h n", n=DH),
                                        PJ[:, u % 2, :].rearrange("p (t h n) -> p t h n", t=T, n=DH),
                                        rstd[:, 0:16].rearrange("p (t h) -> p t h", t=T).unsqueeze(3)
                                        .to_broadcast([P, T, 4, DH]), ALU.mult).then_inc(unit_free[u % 2], 1)
            dve.wait_ge(gains_turned, 1)
            nc.vector.tensor_copy(colT[:, KD:2 * KD + 2], SBK[:, 0, KD:2 * KD + 2]).then_inc(gains_ready, 1)
            dve.wait_ge(gains_ready, 1)
            w_low(8)
            for n in range(2 * HP):
                turned_qk(n)
            w_low(9)
            for g in range(G):
                u = U_BASE + g
                if g % 2:
                    w_low(10 + g // 2)
                dve.wait_ge(mixed, g + 1)
                dve.wait_ge(unit_free[u % 2], u // 2 + 1)
                if g:
                    dve.wait_ge(sgu_ready, g)
                link(nc.vector.tensor_tensor(gated.rearrange("p (n t) -> p n t", t=P),
                                             SBK[:, g % 2, :].rearrange("p (n t) -> p n t", t=P),
                                             sgb[:, g, :].unsqueeze(1).to_broadcast([P, T, P]), ALU.add))
                nc.vector.tensor_tensor(uT[:, g, :], gated, uT[:, g, :], ALU.mult).then_inc(sgu_ready, 1)

            dve.wait_ge(sgu_ready, G)

            def attend(s):
                if s < T * H:
                    h, t = divmod(s, T)
                    n = (t + 1) * P
                    dve.wait_ge(scores_ready, s + 1)
                    dve.wait_ge(relM_ready, h + 1)
                    if s >= 2:
                        dve.wait_ge(exp_ready, s - 1)
                    nc_max = nc.vector.tensor_tensor_reduce(
                        srow[:, s % 2, 0:n], SBK[:, s % 2, 0:n], relM[:, h % 2, 0:n][:, ::-1], 1.0, -3e38,
                        ALU.add, ALU.max, smax[:, s % 2:s % 2 + 1])
                    link(nc_max)
                    nc.vector.tensor_scalar(nmax[:, s % 2:s % 2 + 1], smax[:, s % 2:s % 2 + 1], -1.0, None,
                                            ALU.mult).then_inc(smax_ready, 1)
                if 1 <= s <= T * H:
                    a, n = s - 1, ((s - 1) % T + 1) * P
                    dve.wait_ge(exp_ready, a + 1)
                    link(nc.vector.reciprocal(rsum[:, a % 2:a % 2 + 1], ssum[:, a % 2:a % 2 + 1]))
                    nc.vector.tensor_scalar(prow[:, a % 2, 0:n], prow[:, a % 2, 0:n], rsum[:, a % 2:a % 2 + 1], None,
                                            ALU.mult).then_inc(probs_ready, 1)

            def merge(u):
                n, m = u - B_BASE, (u - B_BASE) % KD
                if A_BASE < u < O_BASE - 1 and u % 2:
                    w_low(10 + (u - U_BASE) // 2)
                dve.wait_ge(gate_ready, n + 1)
                if n < KD:
                    nc.vector.tensor_tensor(merged[:, m, :], gate[:, n % 2, :], PJ[:, u % 2, 512:1024],
                                            ALU.mult).then_inc(unit_free[u % 2], 1)
                    dve.wait_ge(unit_free[u % 2], u // 2 + 1)
                    nc.vector.engine_nop().then_inc(merged_ready, 1)
                else:
                    dve.wait_ge(merged_ready, n)
                    nc.vector.tensor_tensor(gated, gate[:, n % 2, :], PJ[:, u % 2, 512:1024],
                                            ALU.mult).then_inc(unit_free[u % 2], 1)
                    dve.wait_ge(unit_free[u % 2], u // 2 + 1)
                    nc.vector.tensor_tensor(merged[:, m, :], merged[:, m, :], gated, ALU.add).then_inc(merged_ready, 1)

            for s in range(T * H + 1):
                attend(s)
                if 8 < s < T * H and s % 8 == 1:
                    w_low(11 + s // 8)
                if s < T * H and s % 4 == 3:
                    merge(B_BASE + s // 4)
            for m in range(KD):
                merge(A_BASE + m)
                if m == 0:
                    w_low(BEFORE_A)
                dve.wait_ge(merged_ready, KD + m + 1)
                dve.wait_ge(m_hi_ready, m + 1)
                nc.vector.tensor_tensor(m_lo[:, m, :], merged[:, m, :], m_hi[:, m, :].bitcast(F32),
                                        ALU.subtract).then_inc(m_split, 1)
            w_low(N_SPLIT - 3)
            be = [P, T, E]
            dve.wait_ge(pool_made, 19)
            link(nc.vector.tensor_copy(ones_b[:], ones[:]))
            link(nc.vector.tensor_copy(before_b[:], before_m[:]))
            link(nc.vector.tensor_copy(vals[:, :, :, 0], tile_0[:].unsqueeze(2).to_broadcast(be)))
            link(nc.vector.tensor_copy(vals[:, :, :, 1], tokn[:, 0:1].unsqueeze(2).to_broadcast(be)))
            dve.wait_ge(x_again, 16 * T)
            for c in range(4):
                u = O_BASE + c
                dve.wait_ge(unit_ready, u + 1)
                part = x2[:, :, c * PAIRC:(c + 1) * PAIRC]
                nc.vector.tensor_tensor(part, part, t_major(PJ[:, u % 2, :]), ALU.add).then_inc(x2_ready, 1)
                dve.wait_ge(x2_ready, c + 1)
                if c:
                    dve.wait_ge(x2_sq, c)
                for t in range(T):
                    sq = nc.vector.tensor_tensor_reduce(scratch[:, t * PAIRC:(t + 1) * PAIRC], part[:, t, :], part[:, t, :],
                                                        1.0, 0.0, ALU.mult, ALU.add, stat[:, 4 * c + t:4 * c + t + 1])
                sq.then_inc(x2_sq, 1)
                if c < 2:
                    w_low(N_SPLIT - 2 + c)
            dve.wait_ge(x2_sq, 4)
            nc.vector.tensor_reduce(mean[:, 0:T], stat[:, 0:16].rearrange("p (c t) -> p t c", t=T), AX_X,
                                    ALU.add).then_inc(x2_var, 1)
            dve.wait_ge(x2_std, 1)
            nc.vector.reciprocal(rstd[:, 0:T], rstd[:, 0:T]).then_inc(x2_rstd, 1)
            dve.wait_ge(x2_rstd, 1)
            dve.wait_ge(late_in, 32)
            dve.wait_ge(logits_ready, 1)
            link(nc.vector.tensor_tensor(logits, TT[:, 0:TE].rearrange("p (t e) -> p t e", t=T),
                                         rstd[:, 0:T].unsqueeze(2).to_broadcast(be), ALU.mult))
            link(nc.vector.tensor_tensor(logits, logits, rb_all.unsqueeze(1).to_broadcast(be), ALU.add))
            for t in range(T):
                link(nc.vector.max(top[:, t, :], logits[:, t, :]))
                link(nc.vector.max_index(top_i[:, t, :], top[:, t, :], logits[:, t, :]))
            link(nc.vector.tensor_scalar(neg_t, top[:, :, 0], -1.0, None, ALU.mult))
            nc.vector.tensor_copy(top_f, top_i).then_inc(top_ready, 1)
            dve.wait_ge(top_ready, 1)
            all_ranks = [P, T, TOPK, E]
            link(nc.vector.tensor_tensor(hits, iota_e.unsqueeze(1).unsqueeze(1).to_broadcast(all_ranks),
                                         top_f[:, :, 0:TOPK].unsqueeze(3).to_broadcast(all_ranks), ALU.is_equal))
            with nc.allow_low_precision("ones and zeros are exact in bf16"):
                nc.vector.tensor_reduce(chosen[:, :, :], hits.rearrange("p t k e -> p t e k"), AX_X,
                                        ALU.add).then_inc(chosen_ready, 1)
            dve.wait_ge(chosen_ready, 1)
            dve.wait_ge(top_exp, T)
            link(nc.vector.reciprocal(psum_t, psum_t))
            link(nc.vector.tensor_tensor(prob, prob, psum_t.unsqueeze(2).to_broadcast([P, T, TOPK]), ALU.mult))
            link(nc.vector.tensor_tensor(hits, hits, prob.unsqueeze(3).to_broadcast(all_ranks), ALU.mult))
            link(nc.vector.tensor_reduce(weight, hits.rearrange("p t k e -> p t e k"), AX_X, ALU.add))
            link(nc.vector.tensor_copy(vals[:, :, :, 2], weight))
            link(nc.vector.tensor_tensor(hit, weight, vals[:, :, :, 2], ALU.subtract))
            link(nc.vector.tensor_copy(vals[:, :, :, 3], hit))
            link(nc.vector.tensor_tensor(vals[:, :, :, 4], hit, vals[:, :, :, 3], ALU.subtract))
            dve.wait_ge(counted, 1)
            link(nc.vector.tensor_tensor(place_a, tokn[:].unsqueeze(2).to_broadcast(be),
                                         SBK[:, 1, TE:TE + E].unsqueeze(1).to_broadcast(be), ALU.add))
            earlier = SBK[:, 1, 0:TE].rearrange("p (t e) -> p t e", t=T)
            link(nc.vector.tensor_tensor(place_a, place_a, earlier, ALU.subtract))
            link(nc.vector.tensor_tensor(before, earlier, place_a, ALU.subtract))
            link(nc.vector.tensor_tensor(before, before, chosen[:, :, :], ALU.mult))
            link(nc.vector.tensor_tensor(pos[:, :, :], before, place_a, ALU.add))
            nc.vector.tensor_copy(table[0:1, 0:E], SBK[0:1, 1, TE:TE + E]).then_inc(counts_there, 1)
            dve.wait_ge(counts_there, 1)
            def plan(e, size, item, base, at, slots=None):
                blocks = SIZES[size]
                for n_, (b, _) in enumerate(blocks):
                    of_block = slots[b] if slots is not None else {128: slots_128[:, 0:P], 64: slots_64, 32: slots_32}[b]
                    for t in range(T):
                        nc.vector.tensor_scalar(onehot[:, n_, t, :], of_block, pos[:, t, bass.ds(e, 1)], None,
                                                ALU.is_equal)
                nc.vector.tensor_copy(val_e[:, :, :], vals[:, :, bass.ds(e, 1), :].rearrange("p t o c -> p t (o c)")) \
                    .then_inc(hot_ready, 1)
                dve.wait_ge(plan_there, item + 1)
                found = YD[:, 0:2 * VALS].rearrange("p (b c) -> p b c", c=VALS)
                nc.vector.tensor_reduce(plan_w[:, 0:2], found[:, :, 2:5], AX_X, ALU.add)
                nc.vector.tensor_reduce(tok_f[:], found[:, :, 0:2], AX_X, ALU.add).then_inc(dve_chain, 1)
                dve.wait_ge(dve_chain, base + at + 1)
                if size == P:
                    last = nc.vector.tensor_copy(plan_i[:, 0:1], tok_f[:, 0:1])
                else:
                    for n_, (b, _) in enumerate(blocks):
                        last = nc.vector.tensor_scalar(plan_i[:, n_:n_ + 1], tok_f[:, n_:n_ + 1], float(P // b),
                                                       copy_no[:, n_:n_ + 1], ALU.mult, ALU.add)
                last.then_inc(plan_ready, 1)

            PLAN_0 = made[0]
            by_rows(dve, load(dve, N_AT, S), lambda size: plan(0, size, 0, PLAN_0, 0))
            made[0] += 1
            link(nc.vector.tensor_copy(col_cnt, SBK[0:E, 1, TE + E:TE + E + 1]))
            for b in range(3):
                link(nc.vector.tensor_scalar(col_fl[:, b:b + 1], col_cnt, float((b + 1) * P), None, ALU.is_gt))
            link(nc.vector.tensor_reduce(col_nb, col_fl, AX_X, ALU.add))
            link(nc.vector.memset(col_eb[:, 0:2], 0.0))
            nc.vector.tensor_copy(col_eb[:, 0:1], tokn[0:E, 0:1]).then_inc(extra_cols, 1)
            dve.wait_ge(extra_base, 1)
            link(nc.vector.tensor_copy(col_base, TT[0:E, 512:513]))
            for b in range(3):
                link(nc.vector.tensor_scalar(col_code, col_base, float(b), None, ALU.add))
                link(nc.vector.tensor_scalar(oh_x[:, b, :], iota_e[0:E, 0:EXTRA + 1], col_code, col_fl[:, b:b + 1],
                                             ALU.is_equal, ALU.mult))
            link(nc.vector.memset(col_eb[:, 1:2], 1.0))
            nc.vector.engine_nop().then_inc(extra_hot, 1)
            dve.wait_ge(extra_ready, 1)
            J = EXTRA + 1
            link(nc.vector.tensor_copy(table[0:1, XE_AT:XE_AT + J], TT[0:1, 528:528 + J]))
            link(nc.vector.tensor_copy(table[0:1, XB_AT:XB_AT + J], TT[0:1, 544:544 + J]))
            nc.vector.tensor_copy(table[0:1, NX_AT:NX_AT + 1], TT[0:1, 560:561]).then_inc(routed, 1)
            dve.wait_ge(routed, 1)
            BASE = made[0]


            def shift_plan(base, at):
                nc.vector.tensor_copy(plan_w[:, 2:4], plan_w[:, 0:2]).then_inc(dve_chain, 1)
                nc.vector.tensor_copy(plan_i[:, 2:4], plan_i[:, 0:2]).then_inc(dve_chain, 1)
                dve.wait_ge(dve_chain, base + at + 2)

            def take_plan(item, first=False):
                if not first:
                    dve.wait_ge(scattered, item * 32)
                nc.vector.tensor_copy(plan_w[:, 4:6], plan_w[:, 2:4])
                nc.vector.tensor_copy(plan_i[:, 4:6], plan_i[:, 2:4]).then_inc(plan_taken, 1)

            def turned_in(item):
                def go(size):
                    dve.wait_ge(xg_turned, item + 1)
                    for n_, (b, off) in enumerate(SIZES[size]):
                        J, w = P // b, D * b // P
                        C = KD // J
                        gains = colT[:, KD + 2:2 * KD + 2].rearrange("p (j c) -> p c j", c=C)
                        x_, y_ = (a[:, off:off + w].rearrange("p (c j n) -> p c j n", j=J, n=b) for a in (xt, YD))
                        last = nc.vector.tensor_tensor(x_, y_, gains.unsqueeze(3).to_broadcast([P, C, J, b]), ALU.mult)
                    last.then_inc(xT_ready, 1)
                return go

            def lift(item):
                def go(size):
                    for n_, (blk, c0, w) in enumerate(ROUNDS[size]):
                        o = SIZES[size][blk][1] + c0
                        if n_ == 0:
                            dve.wait_ge(gu_ready, item + 1)
                        nc.vector.tensor_copy(us[:, o:o + w], PJ[:, 1, o:o + w]).then_inc(us_ready, 1)
                return go

            def finish(e, item, base, at):
                def go(size):
                    c = at

                    def link_(ins):
                        nonlocal c
                        c += 1
                        ins.then_inc(dve_chain, 1)
                        dve.wait_ge(dve_chain, base + c)

                    for n_, (blk, c0, w) in enumerate(ROUNDS[size]):
                        b, off = SIZES[size][blk]
                        o, J = off + c0, P // b
                        C = FT // J

                        def tiles(ap):
                            return ap.rearrange("p (c j n) -> p c j n", j=J, n=b)

                        def bias(which):
                            cols = bguT[:, bass.ds(e * (2 * FT) + which * FT, FT)].rearrange("p (j c) -> p c j", c=C)
                            return cols[:, c0 // P:(c0 + w) // P, :].unsqueeze(3).to_broadcast([P, w // P, J, b])

                        g_at, u_at = turned_at(size, n_)
                        g, u, s, h = (a[:, o:o + w] for a in (eg, eu, es, hh))
                        dve.wait_ge(turned, item * 2 + (n_ + 1))
                        link_(nc.vector.tensor_tensor(tiles(g), tiles(TT[:, g_at:g_at + w]), bias(0), ALU.add))
                        nc.vector.tensor_scalar(g, g, LIMIT, None, ALU.min).then_inc(g_ready, 1)
                        nc.vector.tensor_tensor(tiles(u), tiles(TT[:, u_at:u_at + w]), bias(1),
                                                ALU.add).then_inc(turned_read, 1)
                        dve.wait_ge(turned_read, item * 2 + (n_ + 1))
                        link_(nc.vector.tensor_scalar(u, u, LIMIT, -LIMIT, ALU.min, ALU.max))
                        dve.wait_ge(g_ready, item * 2 + (n_ + 1))
                        link_(nc.vector.scalar_tensor_tensor(u, u, 1.0, g, ALU.add, ALU.mult))
                        dve.wait_ge(s_ready, item * 2 + (n_ + 1))
                        nc.vector.tensor_tensor(h, u, s, ALU.mult).then_inc(hh_ready, 1)
                    assert c - at == 6
                return go

            n0, n1 = load(dve, N_AT, S), load(dve, N_AT + 1, S)
            B0 = BASE
            dve.wait_ge(plan_ready, 1)
            shift_plan(B0, 0)
            dve.wait_ge(gathered, 32)
            by_rows(dve, n0, turned_in(0))
            by_rows(dve, n1, lambda size: plan(1, size, 1, B0, 2))
            for t in range(T):
                dve.wait_ge(bias_added, t + 1)
                nc.vector.tensor_tensor(x2[:, t, :], x2[:, t, :], TT[:, :], ALU.add).then_inc(biased, 1)
            by_rows(dve, n0, lift(0))
            by_rows(dve, n1, turned_in(1))
            by_rows(dve, n0, finish(0, 0, B0, 3))
            take_plan(0, first=True)
            STEP = 9
            with dve.Fori(1, E - 1) as i:
                base = i * STEP + B0
                n, nn = load(dve, i + N_AT, S), load(dve, i + (N_AT + 1), S)
                dve.wait_ge(plan_taken, i)
                dve.wait_ge(plan_ready, i + 1)
                shift_plan(base, 0)
                dve.wait_ge(gathered, i * 32 + 32)
                settle(dve)
                by_rows(dve, nn, lambda size: plan(i + 1, size, i + 1, base, 2))
                by_rows(dve, n, lift(i))
                by_rows(dve, nn, turned_in(i + 1))
                by_rows(dve, n, finish(i, i, base, 3))
                take_plan(i)
            base = (E - 1) * STEP + B0
            dve.wait_ge(plan_taken, E - 1)
            dve.wait_ge(plan_ready, E)
            shift_plan(base, 0)

            def plan_extra(b, item, base, at):
                e, nb, n = load(dve, b + XE_AT, E - 1), load(dve, b + XB_AT, 3), rows_left(dve, b)
                for had, moved in ((slots_64, more_64), (slots_32, more_32)):
                    ins = nc.vector.tensor_scalar(moved, had, slots_128[:, bass.ds(nb * P, 1)], None, ALU.add)
                ins.then_inc(dve_chain, 1)
                dve.wait_ge(dve_chain, base + (at + 1))
                settle(dve)
                slots = {128: slots_128[:, bass.ds(nb * P, P)], 64: more_64, 32: more_32}
                by_rows(dve, n, lambda size: plan(e, size, item, base, at + 1, slots=slots))

            dve.wait_ge(gathered, 32 * E)
            plan_extra(0, E, base, 2)
            by_rows(dve, load(dve, N_AT + E - 1, S),
                    lambda size: (lift(E - 1)(size), finish(E - 1, E - 1, base, 4)(size)))
            take_plan(E - 1)
            MORE = 10
            B2 = base + MORE
            n_extra = load(dve, NX_AT, EXTRA)
            with dve.Fori(0, EXTRA) as b:
                with dve.If(b < n_extra):
                    e, n = load(dve, b + XE_AT, E - 1), rows_left(dve, b)
                    base = b * MORE + B2
                    dve.wait_ge(plan_taken, b + E)
                    dve.wait_ge(plan_ready, b + (E + 1))
                    shift_plan(base, 0)
                    dve.wait_ge(gathered, b * 32 + (E + 1) * 32)
                    settle(dve)
                    by_rows(dve, n, turned_in(b + E))
                    plan_extra(b + 1, b + (E + 1), base, 2)
                    by_rows(dve, n, lambda size: (lift(b + E)(size), finish(e, b + E, base, 4)(size)))
                    take_plan(b + E)
                with dve.Else():
                    dve.nop()

        @block.tensor
        def _(pe):
            mm = nc.tensor.matmul

            def have(c):
                pe.wait_ge(raw_in[slot(c)], 16 * (c // RAW + 1))

            def wchunk(c, n):
                return raw[:, slot(c), :].rearrange("p (k n) -> p k n", n=n)

            def split_chunk(c):
                return [w[:, split_number(c) % 2, :].rearrange("p (k n) -> p k n", n=PAIRC) for w in (w_hi, w_lo)]

            PARTS = ((0, 0), (0, 1), (1, 0))
            hT, m_parts = (hT_hi, hT_lo), (m_hi, m_lo)

            pe.wait_ge(pool_made, 3)
            pe.wait_ge(rows_in, 16)
            nc.tensor.transpose(SBK[:, 0, 0:KD], rows[0:KD, :], ident[0:KD, 0:KD]).then_inc(cols_turned, 1)
            for t in range(T):
                pe.wait_ge(xs_ready, t + 1)
                if t >= 2:
                    pe.wait_ge(h_full_ready, t - 1)
                for k in range(KD):
                    last = nc.tensor.transpose((PJ[:, 1, :] if t % 2 else TT)[:, k * P:(k + 1) * P],
                                               xin[:, t, k * P:(k + 1) * P], ident[:])
                last.then_inc(x_turned, 1)

            def start_unit(u):
                pe.wait_ge(w_split, split_number(UNIT_CHUNK[u]) + 1)
                if u >= 2:
                    pe.wait_ge(unit_free[u % 2], free_before(u))

            def by_tokens(u, lhs):
                if u < O_BASE + 2:
                    start_unit(u)
                else:
                    pe.wait_ge(w_split, split_number(UNIT_CHUNK[u]) + 1)
                    pe.wait_ge(x2_ready, u - O_BASE - 1)
                w = split_chunk(UNIT_CHUNK[u])
                for t in range(T):
                    dst, at = PJ[:, u % 2, t * PAIRC:(t + 1) * PAIRC], slice(t * P, (t + 1) * P)
                    if u == 0:
                        pe.wait_ge(hT_ready, t + 1)
                    for k in range(KD):
                        if u == O_BASE and t == 0:
                            pe.wait_ge(m_split, k + 1)
                        for a, b in PARTS:
                            last = mm(dst, lhs[a][:, k, at], w[b][:, k, :], start=(k == 0 and (a, b) == PARTS[0]),
                                      stop=(k == KD - 1 and (a, b) == PARTS[-1]))
                last.then_inc(unit_ready, 1)

            def turn_qk(n):
                is_k, hp = divmod(n, HP)
                if n >= 2:
                    pe.wait_ge(qk_ready, n - 1)
                for t in range(T):
                    last = nc.tensor.transpose(SBK[:, n % 2, t * P:(t + 1) * P],
                                               qk_rows[is_k][:, t, hp * P:(hp + 1) * P], ident[:])
                last.then_inc(qk_turned, 1)

            for u in range(8):
                by_tokens(u, hT)
                if u == 3:
                    pe.wait_ge(gains_in, 16 * 5)
                    pe.wait_ge(cols_ready, 1)
                    nc.tensor.transpose(SBK[:, 0, 0:2 * KD + 2], rows[0:2 * KD + 2, :],
                                        ident[0:2 * KD + 2, 0:2 * KD + 2]).then_inc(gains_turned, 1)
                    pe.wait_ge(bias_in, 16)
                    for c in range(4):
                        last = nc.tensor.transpose(TT[:, c * P:(c + 1) * P], bias_rows[:, c, :], ident[:])
                    last.then_inc(bias_turned, 1)
                    pe.wait_ge(sgw_masked, 1)
                    for g in range(G):
                        last = nc.tensor.transpose(SBK[:, 1, g * P:(g + 1) * P], sgw_rows[:, g, :], ident[:])
                    last.then_inc(sgw_turned, 1)
                if u == 7:
                    pe.wait_ge(unit_free[1], 3)
                    pe.wait_ge(unit_free[0], 3)
                    pe.wait_ge(gains_ready, 1)
                    pe.wait_ge(wT_ready, 1)
                    for n in range(2 * HP):
                        turn_qk(n)

            def by_features(u, m, ks):
                w = split_chunk(UNIT_CHUNK[u])
                for k in ks:
                    for a, b in PARTS:
                        last = mm(PJ[:, u % 2, 0:512], w[b][:, k, (m % 2) * P:(m % 2 + 1) * P], hT[a][:, k, :],
                                  start=(k == 0 and (a, b) == PARTS[0]), stop=(k == KD - 1 and (a, b) == PARTS[-1]))
                return last

            def branch(u, kind, m, ks, lhs):
                c = BRANCH_CHUNK[(kind, m // 4)]
                have(c)
                w = wchunk(c, 512)
                for k in ks:
                    last = mm(PJ[:, u % 2, 512:1024], w[:, k, (m % 4) * P:(m % 4 + 1) * P], lhs[:, k, :],
                              start=(k == 0), stop=(k == 3))
                return last

            def mix(g):
                if g == 0:
                    pe.wait_ge(vn_ready, 2)
                    pe.wait_ge(qk_ready, 2 * HP)
                if g >= 2:
                    pe.wait_ge(sgu_ready, g - 1)
                for n in range(T):
                    last = mm(SBK[:, g % 2, n * P:(n + 1) * P], vn[:, n, g * P:(g + 1) * P], wT[:, g, :],
                              start=True, stop=True)
                last.then_inc(mixed, 1)

            for m in range(4):
                u = U_BASE + m
                start_unit(u)
                by_features(u, m, range(KD)).then_inc(unit_ready, 1)
                if m:
                    mix(m - 1)
            mix(3)

            def attend(s):
                if s < T * H:
                    h, t = divmod(s, T)
                    rows_ = slice(64 * (h % 2), 64 * (h % 2) + 64)
                    if s >= 2:
                        pe.wait_ge(smax_ready, s - 1)
                    mm(SBK[:, s % 2, 0:(t + 1) * P], qT[rows_, h // 2, t * P:(t + 1) * P], kT[rows_, h // 2, 0:(t + 1) * P],
                       start=True, stop=True).then_inc(scores_ready, 1)
                if 2 <= s < T * H + 2:
                    a = s - 2
                    pe.wait_ge(probs_ready, a + 1)
                    if a:
                        pe.wait_ge(pcol_ready, a)
                    else:
                        pe.wait_ge(bias_ready, 1)
                    for kt in range(a % T + 1):
                        last = nc.tensor.transpose(PT[:, kt * P:(kt + 1) * P], prow[:, a % 2, kt * P:(kt + 1) * P], ident[:])
                    last.then_inc(probs_turned, 1)
                if s >= 3:
                    a = s - 3
                    h, t = divmod(a, T)
                    pe.wait_ge(pcol_ready, a + 1)
                    if a % 8 == 0 and a:
                        pe.wait_ge(attn_ready, a // 8)
                    for kt in range(t + 1):
                        last = mm(PV[64 * (h % 2):64 * (h % 2) + 64, t * P:(t + 1) * P],
                                  vv[:, kt, h * DH:(h + 1) * DH], pcol[:, a % 2, kt * P:(kt + 1) * P],
                                  start=(kt == 0), stop=(kt == t))
                    last.then_inc(pv_done, 1)

            for m in range(KD):
                u = B_BASE + m
                start_unit(u)
                by_features(u, m, range(0, 3))
                if m == 0:
                    pe.wait_ge(sgu_ready, G)
                    pe.wait_ge(bias_ready, 1)
                attend(4 * m)
                by_features(u, m, range(3, 6))
                attend(4 * m + 1)
                by_features(u, m, range(6, 8))
                branch(u, "b", m, range(0, 1), uT)
                attend(4 * m + 2)
                branch(u, "b", m, range(1, 4), uT).then_inc(unit_ready, 1)
                attend(4 * m + 3)
            for m in range(KD):
                u = A_BASE + m
                start_unit(u)
                if m == 0:
                    for s in range(3):
                        by_features(u, m, range(3 * s, min(3 * s + 3, KD)))
                        attend(T * H + s)
                    pe.wait_ge(attn_ready, HP)
                else:
                    by_features(u, m, range(KD))
                branch(u, "a", m, range(4), qT).then_inc(unit_ready, 1)
            def turn_x2(c):
                pe.wait_ge(x2_ready, c + 1)
                for k in (2 * c, 2 * c + 1):
                    if k >= 2:
                        pe.wait_ge(h2T_ready, k - 1)
                    for t in range(T):
                        last = nc.tensor.transpose(SBK[:, k % 2, t * P:(t + 1) * P], x2[:, t, k * P:(k + 1) * P], ident[:])
                    last.then_inc(h2_turned, 1)

            def route(c):
                for k in (2 * c, 2 * c + 1):
                    pe.wait_ge(h2T_ready, k + 1)
                    for t in range(T):
                        last = mm(TT[:, t * E:(t + 1) * E], h2T[:, k, t * P:(t + 1) * P], rw[:, k, :],
                                  start=(k == 0 and t == 0), stop=(k == KD - 1 and t == T - 1))
                return last

            by_tokens(O_BASE, m_parts)
            by_tokens(O_BASE + 1, m_parts)
            turn_x2(0)
            by_tokens(O_BASE + 2, m_parts)
            pe.wait_ge(late_in, 32)
            route(0)
            turn_x2(1)
            by_tokens(O_BASE + 3, m_parts)
            route(1)
            turn_x2(2)
            route(2)
            turn_x2(3)
            route(3).then_inc(logits_ready, 1)
            pe.wait_ge(chosen_ready, 1)
            for t in range(T):
                for s in range(t + 1):
                    mm(SBK[:, 1, t * E:(t + 1) * E], before_b[:] if s == t else ones_b[:], chosen[:, s, :],
                       start=(s == 0), stop=(s == t))
            for t in range(T):
                mm(SBK[:, 1, TE:TE + E], ones_b[:], chosen[:, t, :], start=(t == 0), stop=(t == T - 1))
            for t in range(T):
                last = mm(SBK[0:E, 1, TE + E:TE + E + 1], chosen[:, t, :], ones_b[:, 0:1], start=(t == 0), stop=(t == T - 1))
            last.then_inc(counted, 1)
            pe.wait_ge(counts_there, 1)

            def plan(item):
                pe.wait_ge(hot_ready, item + 1)
                for n_ in range(2):
                    for t in range(T):
                        last = mm(YD[:, VALS * n_:VALS * (n_ + 1)], onehot[:, n_, t, :], val_e[:, t, :], start=(t == 0),
                                  stop=(t == T - 1))
                last.then_inc(plan_there, 1)

            def turn_in(item):
                def go(size):
                    pe.wait_ge(gathered, item * 32 + 32)
                    for b, off in SIZES[size]:
                        for c in range(KD * b // P):
                            at = slice(off + c * P, off + (c + 1) * P)
                            last = nc.tensor.transpose(YD[:, at], xg[:, at], ident[:])
                    last.then_inc(xg_turned, 1)
                return go

            def arrived_in(j, item):
                pe.wait_ge(arrived[j], item * 16 + 16)

            def multiply(dst, lhs, b, off, tile, w, first, last_):
                J = P // b
                W, C = D // J, KD // J
                j_in, c = divmod(tile, C)
                for col in range(0, W, 512):
                    for j in range(J):
                        n = min(W, 512)
                        ins = mm(dst[j * b:(j + 1) * b, off + col:off + col + n],
                                 lhs[:, off + c * P + j_in * b:off + c * P + (j_in + 1) * b],
                                 w[:, j * W + col:j * W + col + n], start=first, stop=last_)
                return ins

            def together(js, size):
                return [js[at:at + 2] for at in range(0, len(js), 2)] if size == 96 else [[j] for j in js]

            def up(item, js):
                def go(size):
                    if js[0] == 0:
                        pe.wait_ge(xT_ready, item + 1)
                    for group in together(js, size):
                        for n_, (b, off) in enumerate(SIZES[size]):
                            for j in group:
                                if n_ == 0:
                                    arrived_in(j, item)
                                for w in range(2):
                                    last = multiply(PJ[:, w, :], xt, b, off, j, ring[:, j, w * FF:(w + 1) * FF],
                                                    j == 0, j == KD - 1)
                                if n_ == len(SIZES[size]) - 1:
                                    last.then_inc({0: first_used, KD - 1: gu_ready}.get(j, chunk_used), 1)
                return go

            def turn(item):
                def go(size):
                    for n_, (blk, c0, w) in enumerate(ROUNDS[size]):
                        o = SIZES[size][blk][1] + c0
                        pe.wait_ge(gs_ready, item * 2 + (n_ + 1))
                        pe.wait_ge(us_ready, item * 2 + (n_ + 1))
                        if n_ and size != 64:
                            pe.wait_ge(turned_read, item * 2 + n_)
                        for at, src in zip(turned_at(size, n_), (gs, us)):
                            for c in range(0, w, P):
                                last = nc.tensor.transpose(TT[:, at + c:at + c + P], src[:, o + c:o + c + P], ident[:])
                        last.then_inc(turned, 1)
                return go

            def down(item):
                def go(size):
                    waited = set()
                    for group in together(range(KD, SLOTS), size):
                        for n_, (b, off) in enumerate(SIZES[size]):
                            for j in group:
                                if n_ == 0:
                                    arrived_in(j, item)
                                for c in range(2):
                                    f = 2 * (j - KD) + c
                                    col = (f % (KD * b // P)) * P
                                    made = [k for k, (blk, c0, w) in enumerate(ROUNDS[size])
                                            if blk == n_ and c0 <= col < c0 + w][0]
                                    if made not in waited:
                                        pe.wait_ge(hh_ready, item * 2 + (made + 1))
                                        waited.add(made)
                                    last = multiply(YD, hh, b, off, f, ring[:, j, c * D:(c + 1) * D], f == 0, f == FT - 1)
                                if n_ == len(SIZES[size]) - 1:
                                    last.then_inc(yd_ready if j == SLOTS - 1 else chunk_used, 1)
                return go

            def item(i, n, nn):
                by_rows(pe, n, up(i, [1]))
                pe.wait_ge(y_ready, i)
                plan(i + 1)
                by_rows(pe, n, up(i, [2, 3, 4, 5, 6, 7]))
                by_rows(pe, nn, turn_in(i + 1))
                by_rows(pe, n, turn(i))
                by_rows(pe, nn, up(i + 1, [0]))
                by_rows(pe, n, down(i))

            n0, n1 = load(pe, N_AT, S), load(pe, N_AT + 1, S)
            plan(0)
            for t in range(T):
                last = nc.tensor.transpose(TT[0:E, t * P:(t + 1) * P], weight[:, t, :], ident[:])
            last.then_inc(weights_turned, 1)
            pe.wait_ge(extra_cols, 1)
            mm(TT[0:E, 512:513], before_m[0:E, 0:E], col_nb, start=True, stop=True).then_inc(extra_base, 1)
            pe.wait_ge(extra_hot, 1)
            J = EXTRA + 1
            for b in range(3):
                mm(TT[0:1, 528:528 + J], col_eb[:, 0:1], oh_x[:, b, :], start=(b == 0), stop=(b == 2))
            for b in range(3):
                for again in range(b + 1):
                    mm(TT[0:1, 544:544 + J], col_eb[:, 1:2], oh_x[:, b, :], start=(b == 0), stop=(b == 2 and again == b))
            mm(TT[0:1, 560:561], col_eb[:, 1:2], col_nb, start=True, stop=True).then_inc(extra_ready, 1)
            by_rows(pe, n0, turn_in(0))
            by_rows(pe, n0, up(0, [0]))
            by_rows(pe, n0, up(0, [1]))
            plan(1)
            pe.wait_ge(routed, 1)
            pe.wait_ge(wTe_ready, 1)
            pe.wait_ge(bd_in, 16)
            for t in range(T):
                by_rows(pe, n0, up(0, [2 + t]))
                if t:
                    pe.wait_ge(biased, t)
                for c in range(2):
                    last = mm(TT[:, c * 512:(c + 1) * 512], wTe[0:E, t * P:(t + 1) * P],
                              bd_rows[0:E, c * 512:(c + 1) * 512], start=True, stop=True)
                last.then_inc(bias_added, 1)
            by_rows(pe, n0, up(0, [6, 7]))
            by_rows(pe, n1, turn_in(1))
            pe.wait_ge(biased, T)
            by_rows(pe, n0, turn(0))
            by_rows(pe, n1, up(1, [0]))
            by_rows(pe, n0, down(0))
            with pe.Fori(1, E - 1) as i:
                item(i, load(pe, i + N_AT, S), load(pe, i + (N_AT + 1), S))
            n = load(pe, N_AT + E - 1, S)
            by_rows(pe, n, up(E - 1, [1]))
            pe.wait_ge(y_ready, E - 1)
            plan(E)
            by_rows(pe, n, lambda size: [step(size) for step in (
                up(E - 1, [2, 3, 4, 5, 6, 7]), turn(E - 1), down(E - 1))])
            n_extra = load(pe, NX_AT, EXTRA)
            with pe.Fori(0, EXTRA) as b:
                with pe.If(b < n_extra):
                    n = rows_left(pe, b)
                    pe.wait_ge(y_ready, b + E)
                    settle(pe)
                    by_rows(pe, n, turn_in(b + E))
                    pe.wait_ge(xT_ready, b + (E + 1))
                    plan(b + (E + 1))
                    by_rows(pe, n, lambda size: [step(size) for step in (
                        up(b + E, list(range(KD))), turn(b + E), down(b + E))])
                with pe.Else():
                    pe.nop()


_INS = ['x', 'norm1_g', 'w_in', 'q_norm_g', 'k_norm_g', 'rel_bias', 'sg_ln_g', 'sg_ln_b', 'sg_w', 'sg_b',
        'w_branch_a', 'w_branch_b', 'w_out', 'norm2_g', 'router_w', 'router_b',
        'w_gate_up', 'b_gate_up', 'w_down', 'b_down']


def kernel(**inputs):
    import numpy as _np
    import concourse.bacc as _bacc
    from concourse import mybir as _mybir
    from concourse.bass_utils import run_bass_kernel_spmd as _run

    nc = _bacc.Bacc("TRN2", target_bir_lowering=False, num_devices=1)
    arrays, args = {}, []
    for name in _INS:
        a = _np.ascontiguousarray(inputs[name])
        arrays[f"in_{name}_dram"] = a
        args.append(nc.dram_tensor(f"in_{name}_dram", a.shape, _mybir.dt.from_np(a.dtype), kind="ExternalInput").ap())
    shape = inputs['x'].shape
    args.append(nc.dram_tensor("out_0_dram", shape, _mybir.dt.from_np(_np.dtype('float32')), kind="ExternalOutput").ap())
    block_kernel(nc, *args)
    r = _run(nc, [arrays], core_ids=[0])
    return r.results[0]["out_0_dram"]
```
